# Optimizing a Trainium2 kernel written in Bass

```python
import jax, jax.numpy as jnp
from jax import lax
import numpy as np

D_MODEL = 1024
BATCH = 1
SEQ = 1024
DEPTH = 1

SB_HEADS = 8
SB_HEAD_DIM = 64
SB_WIDTH = SB_HEADS * SB_HEAD_DIM
SB_BLOCK = 128
ML_HEADS = 4
ML_HEAD_DIM = 128
ML_WIDTH = ML_HEADS * ML_HEAD_DIM
ML_CHUNK = 64
CONV_WIDTH = 4
PEER_HEADS = 8
PEER_N_KEYS = 128
PEER_N_EXPERTS = PEER_N_KEYS * PEER_N_KEYS
PEER_QUERY_DIM = 256
PEER_HALF = PEER_QUERY_DIM // 2
PEER_TOPK = 16
PEER_TOKEN_BLOCK = 128

RMS_EPS = 1e-6

O_SB = 3 * SB_WIDTH
O_MLQK = O_SB + 2 * ML_WIDTH
O_MLV = O_MLQK + ML_WIDTH
O_MLO = O_MLV + ML_WIDTH
O_MLIF = O_MLO + 2 * ML_HEADS
IN_COLS = O_MLIF + 2 * D_MODEL

kernel_name = 'hybrid_sba_mlstm_peer'

def rmsnorm(x, w):
    xf = x.astype(jnp.float32)
    y = xf * lax.rsqrt(jnp.mean(xf * xf, axis=-1, keepdims=True) + RMS_EPS) * w.astype(jnp.float32)
    return y.astype(x.dtype)

def causal_short_conv(x, w, b):
    K = w.shape[0]
    S = x.shape[1]
    xp = jnp.pad(x, ((0, 0), (K - 1, 0), (0, 0)))
    y = xp[:, 0:S] * w[0]
    for j in range(1, K):
        y = y + xp[:, j:j + S] * w[j]
    return y + b

def stick_breaking_attention(q, k, v):
    S = q.shape[2]
    scale = SB_HEAD_DIM ** -0.5
    outs = []
    for blk in range(S // SB_BLOCK):
        start = blk * SB_BLOCK
        end = start + SB_BLOCK
        qb = q[:, :, start:end]
        kb = k[:, :, :end]
        vb = v[:, :, :end]
        z = jnp.einsum('bhtd,bhsd->bhts', qb, kb) * scale
        t_pos = start + jnp.arange(SB_BLOCK)[:, None]
        s_pos = jnp.arange(end)[None, :]
        causal = s_pos < t_pos
        sp = jnp.where(causal, jax.nn.softplus(z), 0.0)
        sp_next = jnp.concatenate([sp[..., 1:], jnp.zeros_like(sp[..., :1])], axis=-1)
        suffix = lax.cumsum(sp_next, axis=3, reverse=True)
        w = jnp.where(causal, jnp.exp(jax.nn.log_sigmoid(z) - suffix), 0.0)
        outs.append(jnp.einsum('bhts,bhsd->bhtd', w, vb))
    return jnp.concatenate(outs, axis=2)

def _to_chunks(a):
    B, H, S = a.shape[:3]
    a = a.reshape((B, H, S // ML_CHUNK, ML_CHUNK) + a.shape[3:])
    return jnp.moveaxis(a, 2, 0)

def mlstm_chunkwise(q, k, v, i_pre, f_pre):
    B, H, S, D = q.shape
    logf = jax.nn.log_sigmoid(f_pre)
    tri = jnp.tril(jnp.ones((ML_CHUNK, ML_CHUNK), dtype=bool))

    def step(carry, inp):
        C, n, m = carry
        qc, kc, vc, ic, lfc = inp
        b = jnp.cumsum(lfc, axis=-1)
        dmat = jnp.where(tri, b[..., :, None] - b[..., None, :] + ic[..., None, :], -jnp.inf)
        inter = b + m[..., None]
        m_t = jnp.maximum(inter, jnp.max(dmat, axis=-1))
        w_intra = jnp.exp(dmat - m_t[..., None])
        w_inter = jnp.exp(inter - m_t)
        s = jnp.einsum('bhtd,bhsd->bhts', qc, kc) * w_intra
        num = jnp.einsum('bhts,bhsd->bhtd', s, vc) + w_inter[..., None] * jnp.einsum('bhtd,bhde->bhte', qc, C)
        den = jnp.sum(s, axis=-1) + w_inter * jnp.einsum('bhtd,bhd->bht', qc, n)
        h = num / jnp.maximum(jnp.abs(den), jnp.exp(-m_t))[..., None]
        b_last = b[..., -1]
        g = b_last[..., None] - b + ic
        m_new = jnp.maximum(b_last + m, jnp.max(g, axis=-1))
        decay = jnp.exp(b_last + m - m_new)
        wk = jnp.exp(g - m_new[..., None])
        C_new = decay[..., None, None] * C + jnp.einsum('bhs,bhsd,bhse->bhde', wk, kc, vc)
        n_new = decay[..., None] * n + jnp.einsum('bhs,bhsd->bhd', wk, kc)
        return (C_new, n_new, m_new), h

    init = (jnp.zeros((B, H, D, D), jnp.float32), jnp.zeros((B, H, D), jnp.float32), jnp.zeros((B, H), jnp.float32))
    xs = (_to_chunks(q), _to_chunks(k), _to_chunks(v), _to_chunks(i_pre), _to_chunks(logf))
    _, hs = lax.scan(step, init, xs)
    return jnp.moveaxis(hs, 0, 2).reshape(B, H, S, D)

def hybrid_mixer(xn, w_in, conv_w, conv_b, b_igate, b_fgate, mlstm_norm_w, w_branch_sb, w_branch_ml, w_out):
    B, S, _ = xn.shape
    proj = xn @ w_in
    sb_qkv, ml_qk, ml_v, ml_o, ml_if, gates = jnp.split(proj, [O_SB, O_MLQK, O_MLV, O_MLO, O_MLIF], axis=-1)

    sb = sb_qkv.astype(jnp.float32).reshape(B, S, 3, SB_HEADS, SB_HEAD_DIM).transpose(2, 0, 3, 1, 4)
    y_sb = stick_breaking_attention(sb[0], sb[1], sb[2])
    y_sb = y_sb.transpose(0, 2, 1, 3).reshape(B, S, SB_WIDTH)

    qk = jax.nn.silu(causal_short_conv(ml_qk, conv_w, conv_b)).astype(jnp.float32)
    q_m, k_m = jnp.split(qk, 2, axis=-1)
    to_heads = lambda a: a.reshape(B, S, ML_HEADS, ML_HEAD_DIM).transpose(0, 2, 1, 3)
    q_m = to_heads(q_m)
    k_m = to_heads(k_m) * (ML_HEAD_DIM ** -0.5)
    v_m = to_heads(ml_v.astype(jnp.float32))
    ml_if = ml_if.astype(jnp.float32)
    i_pre = (ml_if[..., :ML_HEADS] + b_igate.astype(jnp.float32)).transpose(0, 2, 1)
    f_pre = (ml_if[..., ML_HEADS:] + b_fgate.astype(jnp.float32)).transpose(0, 2, 1)
    h = mlstm_chunkwise(q_m, k_m, v_m, i_pre, f_pre)
    h = h * lax.rsqrt(jnp.mean(h * h, axis=-1, keepdims=True) + RMS_EPS) * mlstm_norm_w.astype(jnp.float32).reshape(ML_HEADS, 1, ML_HEAD_DIM)
    y_ml = jax.nn.sigmoid(ml_o.astype(jnp.float32)) * h.transpose(0, 2, 1, 3).reshape(B, S, ML_WIDTH)

    g_sb, g_ml = jnp.split(gates.astype(jnp.float32), 2, axis=-1)
    merged = jax.nn.sigmoid(g_sb) * (y_sb @ w_branch_sb) + jax.nn.sigmoid(g_ml) * (y_ml @ w_branch_ml)
    return (merged @ w_out).astype(xn.dtype)

def peer(xn, w_query, keys1, keys2, expert_u, expert_v):
    B, S, D = xn.shape
    T = B * S
    xt = xn.reshape(T, D)
    q = (xt @ w_query).astype(jnp.float32).reshape(T, PEER_HEADS, 2, PEER_HALF)
    s1 = jnp.einsum('thd,hkd->thk', q[:, :, 0], keys1.astype(jnp.float32))
    s2 = jnp.einsum('thd,hkd->thk', q[:, :, 1], keys2.astype(jnp.float32))
    v1, i1 = lax.top_k(s1, PEER_TOPK)
    v2, i2 = lax.top_k(s2, PEER_TOPK)
    cand = (v1[..., :, None] + v2[..., None, :]).reshape(T, PEER_HEADS, PEER_TOPK * PEER_TOPK)
    top_s, top_c = lax.top_k(cand, PEER_TOPK)
    e_idx = jnp.take_along_axis(i1, top_c // PEER_TOPK, axis=-1) * PEER_N_KEYS + jnp.take_along_axis(i2, top_c % PEER_TOPK, axis=-1)
    gate = jax.nn.softmax(top_s, axis=-1)
    n_sel = PEER_HEADS * PEER_TOPK
    idx = e_idx.reshape(T // PEER_TOKEN_BLOCK, PEER_TOKEN_BLOCK, n_sel)
    gts = gate.reshape(T // PEER_TOKEN_BLOCK, PEER_TOKEN_BLOCK, n_sel)
    xb = xt.reshape(T // PEER_TOKEN_BLOCK, PEER_TOKEN_BLOCK, D)

    def block_fn(args):
        xc, ic, gc = args
        u = expert_u[ic].astype(jnp.float32)
        act = jax.nn.gelu(jnp.einsum('ckd,cd->ck', u, xc.astype(jnp.float32)), approximate=False)
        return jnp.einsum('ck,ckd->cd', gc * act, expert_v[ic].astype(jnp.float32))

    out = lax.map(block_fn, (xb, idx, gts))
    return out.reshape(B, S, D).astype(xn.dtype)

def setup_inputs(seed: int = 0) -> dict:
    key = jax.random.key(seed)
    ks = jax.random.split(key, 18)
    f32 = jnp.float32
    nrm = lambda k, shape: jax.random.normal(k, shape, f32)
    return {
        'x': nrm(ks[0], (BATCH, SEQ, D_MODEL)),
        'norm_mix_w': 1.0 + 0.02 * nrm(ks[1], (DEPTH, D_MODEL)),
        'w_in': nrm(ks[2], (DEPTH, D_MODEL, IN_COLS)) * D_MODEL ** -0.5,
        'conv_w': nrm(ks[3], (DEPTH, CONV_WIDTH, 2 * ML_WIDTH)) * CONV_WIDTH ** -0.5,
        'conv_b': 0.02 * nrm(ks[4], (DEPTH, 2 * ML_WIDTH)),
        'b_igate': 0.1 * nrm(ks[5], (DEPTH, ML_HEADS)),
        'b_fgate': 3.0 + 3.0 * jax.random.uniform(ks[6], (DEPTH, ML_HEADS), f32),
        'mlstm_norm_w': 1.0 + 0.02 * nrm(ks[7], (DEPTH, ML_WIDTH)),
        'w_branch_sb': nrm(ks[8], (DEPTH, SB_WIDTH, D_MODEL)) * SB_WIDTH ** -0.5,
        'w_branch_ml': nrm(ks[9], (DEPTH, ML_WIDTH, D_MODEL)) * ML_WIDTH ** -0.5,
        'w_out': nrm(ks[10], (DEPTH, D_MODEL, D_MODEL)) * D_MODEL ** -0.5,
        'norm_ffn_w': 1.0 + 0.02 * nrm(ks[11], (DEPTH, D_MODEL)),
        'peer_w_query': nrm(ks[12], (DEPTH, D_MODEL, PEER_HEADS * PEER_QUERY_DIM)) * D_MODEL ** -0.5,
        'peer_keys1': nrm(ks[13], (DEPTH, PEER_HEADS, PEER_N_KEYS, PEER_HALF)) * PEER_HALF ** -0.5,
        'peer_keys2': nrm(ks[14], (DEPTH, PEER_HEADS, PEER_N_KEYS, PEER_HALF)) * PEER_HALF ** -0.5,
        'peer_u': nrm(ks[15], (DEPTH, PEER_N_EXPERTS, D_MODEL)) * D_MODEL ** -0.5,
        'peer_v': 0.5 * nrm(ks[16], (DEPTH, PEER_N_EXPERTS, D_MODEL)),
        'norm_final_w': 1.0 + 0.02 * nrm(ks[17], (D_MODEL,)),
    }

def reference(x, norm_mix_w, w_in, conv_w, conv_b, b_igate, b_fgate, mlstm_norm_w, w_branch_sb, w_branch_ml, w_out, norm_ffn_w, peer_w_query, peer_keys1, peer_keys2, peer_u, peer_v, norm_final_w):
    h = x
    for l in range(DEPTH):
        xn = rmsnorm(h, norm_mix_w[l])
        h = h + hybrid_mixer(xn, w_in[l], conv_w[l], conv_b[l], b_igate[l], b_fgate[l], mlstm_norm_w[l], w_branch_sb[l], w_branch_ml[l], w_out[l]).astype(h.dtype)
        hn = rmsnorm(h, norm_ffn_w[l])
        h = h + peer(hn, peer_w_query[l], peer_keys1[l], peer_keys2[l], peer_u[l], peer_v[l]).astype(h.dtype)
    return rmsnorm(h, norm_final_w)


_drawn_inputs = setup_inputs


def setup_inputs(seed=0):
    import zlib

    import numpy as np

    out = dict(_drawn_inputs(seed))
    spreads = {}
    factors = {'conv_b': 3.329, 'b_igate': 8.0, 'mlstm_norm_w': 3.095, 'norm_final_w': 2.878}
    for name, (base, spread) in spreads.items():
        noise = np.random.default_rng([zlib.crc32(name.encode()), seed]).standard_normal(out[name].shape)
        drawn = base * np.exp(spread * noise) if base else spread * noise
        out[name] = __import__('jax').numpy.asarray(drawn.astype(out[name].dtype))
    for name, factor in factors.items():
        out[name] = (out[name] * factor).astype(out[name].dtype)
    return out
```

```python
from contextlib import ExitStack

import numpy as np

import concourse.bass as bass
from concourse import mybir

F32 = mybir.dt.float32
I32 = mybir.dt.int32
U32 = mybir.dt.uint32
ALU = mybir.AluOpType
ACT = mybir.ActivationFunctionType
AX = mybir.AxisListType

P = 128
T = 1024
D = 1024
KD = D // P
TT = T // P
NCH = 512
TC = T // NCH
EPS = 1e-6

SB_HEADS, SB_DIM = 8, 64
PAIRS = SB_HEADS // 2
ML_HEADS, ML_DIM = 4, 128
CONV = 4

PH, NKEYS, TOPK = 8, 128, 16
NSEL = PH * TOPK
QT = 2 * PH

T_MLQ, T_MLK, T_MLO, T_SBQ, T_SBK, N_FEAT = 0, 4, 8, 12, 16, 20
N_CONV = 8

V_NORM1, V_MLNORM, V_HEADMASK, V_BI, V_BF, V_CONV = 0, 8, 12, 14, 15, 16
N_VEC = V_CONV + N_CONV * (CONV + 1)

NEG = -3.0e38
BIG = 1.0e30


def ds(start, size):
    return bass.ds(start, size)


def causal_tiles():
    return [
        (tc, sb, max(0, sb - tc * (NCH // P)) * P)
        for tc in range(TC)
        for sb in range((tc + 1) * (NCH // P))
    ]


def build(nc, xT, x, vecs, w_feat, w_if, w_tok, w_merge, w_out, w_query, keysT, uv, rows, out):
    ctx = ExitStack()
    with ctx:
        def sem(name):
            return ctx.enter_context(nc.semaphore(name))

        waits_passed = sem("waits_passed")

        def tensors():
            return ExitStack()

        def sb(st, name, shape, dt=F32):
            return st.enter_context(nc.sbuf_tensor(name, shape, dt))

        def ps(st, name, shape, dt=F32):
            return st.enter_context(nc.psum_tensor(name, shape, dt))

        def rwait(eng, s, value):
            eng.wait_ge(s, value)
            eng.sem_inc(waits_passed, 1)

        h_dram = nc.dram_tensor("h_scratch", (T, D), F32)
        hn_dram = nc.dram_tensor("hn_scratch", (T, D), F32)

        vec = sb(ctx, "vec", [P, N_VEC])
        ones = sb(ctx, "ones", [P, P])
        eps = sb(ctx, "eps", [P, 1])

        mix_st = ctx.enter_context(tensors())
        xnT = sb(mix_st, "xnT", [P, KD * T])
        featT = sb(mix_st, "featT", [P, N_FEAT * T])
        proj_st = ctx.enter_context(tensors())
        vtok = sb(proj_st, "vtok", [P, TT * 2 * NCH])
        ifrow = sb(proj_st, "ifrow", [ML_HEADS, 2, T])

        with tensors() as st:
            sq = sb(st, "sq", [P, 2, T])
            rstd = sb(st, "rstd", [P, T])
            ssum = ps(st, "ssum", [P, T])
            x_loaded = [sem(f"x_loaded{k}") for k in range(KD)]
            vec_loaded = sem("vec_loaded")
            ones_set = sem("ones_set")
            sq_ready = sem("sq_ready")
            sq_summed = sem("sq_summed")
            std_ready = sem("std_ready")
            rstd_ready = sem("rstd_ready")

            with nc.Block() as block:

                @block.sync
                def _(sp):
                    xv = xT.rearrange("(k p) t -> k p t", p=P)
                    for k in range(KD):
                        sp.dma_start(xnT[:, k * T:(k + 1) * T], xv[k]).then_inc(x_loaded[k], 16)
                    sp.dma_start(vec[:, :], vecs).then_inc(vec_loaded, 16)

                @block.gpsimd
                def _(pool):
                    pool.memset(eps[:, :], EPS)
                    pool.memset(ones[:, :], 1.0).then_inc(ones_set, 1)

                @block.scalar
                def _(act):
                    for k in range(KD):
                        act.wait_ge(x_loaded[k], 16)
                        if k >= 2:
                            act.wait_ge(sq_summed, k - 1)
                        act.activation(sq[:, k % 2, :], xnT[:, k * T:(k + 1) * T], ACT.Square).then_inc(sq_ready, 1)
                    act.wait_ge(sq_summed, KD)
                    act.wait_ge(ones_set, 1)
                    act.activation(rstd[:, :], ssum[:, :], ACT.Sqrt, scale=1.0 / D, bias=eps[:, 0:1]).then_inc(std_ready, 1)

                @block.tensor
                def _(pe):
                    pe.wait_ge(ones_set, 1)
                    for k in range(KD):
                        pe.wait_ge(sq_ready, k + 1)
                        for c in range(TC):
                            last = pe.matmul(ssum[:, c * NCH:(c + 1) * NCH], ones[:, :],
                                             sq[:, k % 2, c * NCH:(c + 1) * NCH], start=k == 0, stop=k == KD - 1)
                        last.then_inc(sq_summed, 1)

                @block.vector
                def _(dve):
                    dve.wait_ge(std_ready, 1)
                    dve.reciprocal(rstd[:, :], rstd[:, :]).then_inc(rstd_ready, 1)
                    dve.wait_ge(rstd_ready, 1)
                    dve.wait_ge(vec_loaded, 16)
                    for k in range(KD):
                        if k == 0:
                            for kk in range(KD):
                                dve.wait_ge(x_loaded[kk], 16)
                        xk = xnT[:, k * T:(k + 1) * T]
                        dve.scalar_tensor_tensor(xk, xk, vec[:, V_NORM1 + k:V_NORM1 + k + 1], rstd[:, :],
                                                 ALU.mult, ALU.mult).then_inc(rstd_ready, 1)

        with tensors() as st:
            wf = sb(st, "wf", [P, 2, KD * P])
            wt = featT[:, T_SBQ * T:N_FEAT * T].rearrange("p (k c) -> p k c", k=KD)
            wif = sb(st, "wif", [P, KD, 2 * ML_HEADS])
            xs = sb(st, "xs", [P, 2, KD, P])
            conv = sb(st, "conv", [P, 2, T])
            pf = ps(st, "pf", [P, 2, TC, NCH])
            pif = ps(st, "pif", [P, 2, TC, NCH])
            wf_loaded = [sem(f"wf_loaded{u}") for u in range(2)]
            wt_loaded, wif_loaded = sem("wt_loaded"), sem("wif_loaded")
            feat_done = sem("feat_done")
            evac_act, evac_dve = sem("evac_act"), sem("evac_dve")
            if_done, if_ready = sem("if_done"), sem("if_ready")
            xs_ready, tok_done = sem("xs_ready"), sem("tok_done")
            tevac_act, tevac_dve = sem("tevac_act"), sem("tevac_dve")
            conv_step, silu_done = sem("conv_step"), sem("silu_done")
            NSTEP = CONV

            with nc.Block() as block:

                @block.sync
                def _(sp):
                    sp.dma_start(wt, w_tok).then_inc(wt_loaded, 16)
                    sp.dma_start(wif[:, :, :], w_if).then_inc(wif_loaded, 16)
                    for u in range(2):
                        sp.dma_start(wf[:, u, :], w_feat[u]).then_inc(wf_loaded[u], 16)
                    with sp.Fori(0, N_FEAT // 2 - 1) as j:
                        for u in range(2):
                            sp.wait_ge(feat_done, j * 2 + (u + 1))
                            sp.dma_start(wf[:, u:u + 1, :], w_feat.rearrange("n p c -> p n c")[:, ds(j * 2 + (u + 2), 1), :]).then_inc(wf_loaded[u], 16)

                @block.gpsimd
                def _(pool):
                    xv = xnT[:, :].rearrange("p (k t) -> p k t", k=KD)
                    for u in range(2):
                        pool.tensor_copy(xs[:, u, :, :], xv[:, :, u * P:(u + 1) * P]).then_inc(xs_ready, 1)
                    with pool.Fori(0, TT // 2 - 1) as j:
                        for u in range(2):
                            rwait(pool, tok_done, j * 2 + (u + 1))
                            pool.tensor_copy(xs[:, u, :, :], xv[:, :, ds(j * (2 * P) + (u + 2) * P, P)]).then_inc(xs_ready, 1)

                @block.tensor
                def _(pe):
                    pe.wait_ge(wt_loaded, 16)
                    with pe.Fori(0, TT // 2) as j:
                        for u in range(2):
                            pe.wait_ge(xs_ready, j * 2 + (u + 1))
                            pe.wait_ge(tevac_act, j * 2 + (u + 1))
                            pe.wait_ge(tevac_dve, j * 2 + (u + 1))
                            for n in range(2):
                                for k in range(KD):
                                    last = pe.matmul(pf[:, u, n, :], xs[:, u, k, :], wt[:, k, n * NCH:(n + 1) * NCH],
                                                     start=k == 0, stop=k == KD - 1)
                            last.then_inc(tok_done, 1)
                    pe.wait_ge(wif_loaded, 16)
                    for g in range(2):
                        for c in range(TC):
                            for k in range(KD):
                                last = pe.matmul(pif[0:ML_HEADS, g, c, :], wif[:, k, g * ML_HEADS:(g + 1) * ML_HEADS],
                                                 xnT[:, k * T + c * NCH:k * T + (c + 1) * NCH],
                                                 start=k == 0, stop=k == KD - 1)
                    last.then_inc(if_done, 1)
                    pe.wait_ge(tevac_act, TT + 2)
                    pe.wait_ge(tevac_dve, TT + 2)
                    with pe.Fori(0, N_FEAT // 2) as j:
                        for u in range(2):
                            pe.wait_ge(wf_loaded[u], j * 16 + 16)
                            pe.wait_ge(evac_act, j * 2 + (u + 1))
                            pe.wait_ge(evac_dve, j * 2 + (u + 1))
                            for c in range(TC):
                                for k in range(KD):
                                    last = pe.matmul(pf[:, u, c, :], wf[:, u, k * P:(k + 1) * P],
                                                     xnT[:, k * T + c * NCH:k * T + (c + 1) * NCH],
                                                     start=k == 0, stop=k == KD - 1)
                            last.then_inc(feat_done, 1)

                @block.scalar
                def _(act):
                    act.sem_inc(evac_act, 2)
                    act.sem_inc(tevac_act, 2)
                    with act.Fori(0, TT // 2) as j:
                        for u in range(2):
                            rwait(act, tok_done, j * 2 + (u + 1))
                            act.activation(vtok[:, ds(j * (4 * NCH) + u * 2 * NCH, NCH)], pf[:, u, 0, :], ACT.Copy).then_inc(tevac_act, 1)
                    act.wait_ge(if_done, 1)
                    for g in range(2):
                        act.activation(ifrow[:, g, :], pif[0:ML_HEADS, g, :, :].rearrange("p c n -> p (c n)"), ACT.Identity,
                                       bias=vec[0:ML_HEADS, V_BI + g:V_BI + g + 1]).then_inc(if_ready, 1)

                    def evacuate(j, u, tile0):
                        rwait(act, feat_done, j * 2 + (tile0 + u + 1))
                        act.activation(featT[:, ds(j * (2 * T) + (tile0 + u) * T, NCH)], pf[:, u, 0, :], ACT.Copy).then_inc(evac_act, 1)

                    with act.Fori(0, N_CONV // 2) as j:
                        for u in range(2):
                            evacuate(j, u, 0)
                    with act.Fori(0, N_CONV // 2) as j:
                        for u in range(2):
                            evacuate(j, u, N_CONV)
                            rwait(act, conv_step, j * (2 * NSTEP) + (u + 1) * NSTEP)
                            act.activation(featT[:, ds(j * (2 * T) + (T_MLQ + u) * T, T)], conv[:, u, :], ACT.Silu).then_inc(silu_done, 1)
                    with act.Fori(0, N_FEAT // 2 - N_CONV) as j:
                        for u in range(2):
                            evacuate(j, u, 2 * N_CONV)

                @block.vector
                def _(dve):
                    dve.sem_inc(evac_dve, 2)
                    dve.sem_inc(tevac_dve, 2)
                    dve.sem_inc(silu_done, 2)
                    with dve.Fori(0, TT // 2) as j:
                        for u in range(2):
                            rwait(dve, tok_done, j * 2 + (u + 1))
                            dve.tensor_copy(vtok[:, ds(j * (4 * NCH) + (u * 2 + 1) * NCH, NCH)], pf[:, u, 1, :]).then_inc(tevac_dve, 1)

                    def evacuate(j, u, tile0):
                        rwait(dve, feat_done, j * 2 + (tile0 + u + 1))
                        dve.tensor_copy(featT[:, ds(j * (2 * T) + (tile0 + u) * T + NCH, NCH)], pf[:, u, 1, :]).then_inc(evac_dve, 1)

                    with dve.Fori(0, N_CONV // 2) as j:
                        for u in range(2):
                            evacuate(j, u, 0)
                    dve.wait_ge(evac_dve, N_CONV + 2)
                    dve.wait_ge(evac_act, N_CONV + 2)
                    with dve.Fori(0, N_CONV // 2) as j:
                        for u in range(2):
                            evacuate(j, u, N_CONV)

                            def tap(n, j=j, u=u):
                                return vec[:, ds(j * (2 * (CONV + 1)) + (V_CONV + u * (CONV + 1) + n), 1)]

                            rwait(dve, silu_done, j * 2 + (u + 1))
                            dve.tensor_scalar(conv[:, u, :], featT[:, ds(j * (2 * T) + (T_MLQ + u) * T, T)],
                                              tap(CONV - 1), tap(CONV), ALU.mult, ALU.add).then_inc(conv_step, 1)
                            for n in range(CONV - 1):
                                lag = CONV - 1 - n
                                rwait(dve, conv_step, j * (2 * NSTEP) + (u * NSTEP + n + 1))
                                dve.scalar_tensor_tensor(
                                    conv[:, u, lag:T], featT[:, ds(j * (2 * T) + (T_MLQ + u) * T, T - lag)],
                                    tap(n), conv[:, u, lag:T], ALU.mult, ALU.add).then_inc(conv_step, 1)
                    with dve.Fori(0, N_FEAT // 2 - N_CONV) as j:
                        for u in range(2):
                            evacuate(j, u, 2 * N_CONV)

        with tensors() as st:
            NZ, NSP, NW = 3, 4, 3
            ks = sb(st, "ks", [P, T])
            qz = sb(st, "qz", [P, 2, T])
            vz = sb(st, "vz", [P, TT, 2, P])
            tri = sb(st, "tri", [P, P])
            zero = sb(st, "zero", [P, P])
            maskw = sb(st, "maskw", [P, NCH])
            zsb = sb(st, "zsb", [P, NZ, NCH])
            spl = sb(st, "spl", [P, NSP, NCH])
            wgt = sb(st, "wgt", [P, NW, NCH])
            acc = sb(st, "acc", [P, 2, 2, NCH])
            zp = ps(st, "zp", [P, 2, NCH])
            rp = ps(st, "rp", [P, 2, NCH])
            yp = ps(st, "yp", [P, TC, NCH])
            QB = NCH // P
            items = [(tc, sbk, lo, h) for tc, sbk, lo in
                     sorted(causal_tiles(), key=lambda a: (a[0], -a[1])) for h in range(2)]
            NI = len(items)
            last_blk = [sbk == (tc + 1) * QB - 1 for tc, sbk, lo, h in items]
            n_acc = [sum(it[1] > 0 for it in items[:n + 1]) for n in range(NI)]
            NA = n_acc[-1]
            opens = {tc: min(n for n in range(NI) if items[n][0] == tc) for tc in range(TC)}
            closes = {tc: max(n for n in range(NI) if items[n][0] == tc) for tc in range(TC)}

            masks_set, in_copied = sem("masks_set"), sem("in_copied")
            z_done, z_copied, z_neg = sem("z_done"), sem("z_copied"), sem("z_neg")
            e_done, l_done, sp_done = sem("e_done"), sem("l_done"), sem("sp_done")
            acc_done, r_done, arg_done = sem("acc_done"), sem("r_done"), sem("arg_done")
            w_done, pv_done, y_stored = sem("w_done"), sem("pv_done"), sem("y_stored")
            N_COPY = 5
            N_MASKS = 6

            with nc.Block() as block:

                @block.gpsimd
                def _(pool):
                    pool.memset(vz[:, :, :, :], 0.0).then_inc(masks_set, 1)
                    pool.memset(zero[:, :], 0.0).then_inc(masks_set, 1)
                    pool.memset(tri[:, :], 1.0).then_inc(masks_set, 1)
                    pool.memset(maskw[:, :], 0.0).then_inc(masks_set, 1)
                    pool.wait_ge(masks_set, 4)
                    pool.affine_select(out=tri[:, :], in_=tri[:, :], compare_op=ALU.is_ge, fill=0.0, base=0,
                                       pattern=[[-1, P]], channel_multiplier=1).then_inc(masks_set, 1)
                    pool.affine_select(out=maskw[:, 0:P], in_=maskw[:, 0:P], compare_op=ALU.is_gt, fill=-BIG, base=0,
                                       pattern=[[1, P]], channel_multiplier=-1).then_inc(masks_set, 1)
                    with pool.Fori(0, PAIRS) as hp:
                        for n, (tc, sbk, lo, h) in enumerate(items):
                            if sbk == 0:
                                continue
                            rwait(pool, sp_done, hp * NI + (n + 1))
                            if n >= 2:
                                rwait(pool, r_done, hp * NI + (n - 1))
                            b = sbk % 2
                            if last_blk[n]:
                                pool.tensor_copy(acc[:, h, b, lo:], spl[:, n % NSP, lo:]).then_inc(acc_done, 1)
                                continue
                            prev = items[n - 2][2]
                            rwait(pool, acc_done, hp * NA + n_acc[n - 2])
                            if prev > lo:
                                pool.tensor_copy(acc[:, h, b, lo:prev], spl[:, n % NSP, lo:prev])
                            pool.tensor_tensor(acc[:, h, b, prev:], acc[:, h, 1 - b, prev:], spl[:, n % NSP, prev:],
                                               ALU.add).then_inc(acc_done, 1)

                @block.tensor
                def _(pe):
                    pe.sem_inc(pv_done, 1)
                    pe.wait_ge(masks_set, N_MASKS)
                    with pe.Fori(0, PAIRS) as hp:
                        pe.wait_ge(in_copied, hp * N_COPY + N_COPY)
                        for i in range(NI + 4):
                            if i < NI:
                                tc, sbk, lo, h = items[i]
                                if i >= 2:
                                    pe.wait_ge(z_copied, hp * NI + (i - 1))
                                pe.matmul(zp[:, i % 2, lo:], ks[:, sbk * P:(sbk + 1) * P],
                                          qz[:, h, tc * NCH + lo:(tc + 1) * NCH], start=True, stop=True).then_inc(z_done, 1)
                            if 2 <= i < NI + 2:
                                n = i - 2
                                tc, sbk, lo, h = items[n]
                                pe.wait_ge(sp_done, hp * NI + (n + 1))
                                if n >= 2:
                                    pe.wait_ge(arg_done, hp * NI + (n - 1))
                                last = pe.matmul(rp[:, n % 2, lo:], tri[:, :], spl[:, n % NSP, lo:],
                                                 start=True, stop=last_blk[n])
                                if not last_blk[n]:
                                    prev = items[n - 2][2]
                                    pe.wait_ge(acc_done, hp * NA + n_acc[n - 2])
                                    last = pe.matmul(rp[:, n % 2, prev:], ones[:, :], acc[:, h, 1 - sbk % 2, prev:],
                                                     start=False, stop=True)
                                last.then_inc(r_done, 1)
                            if i >= 4:
                                n = i - 4
                                tc, sbk, lo, h = items[n]
                                if n == opens[tc]:
                                    pe.wait_ge(y_stored, hp * TC + (tc + 1))
                                    pe.matmul(yp[:, tc, :], zero[:, :], qz[:, 0, 0:NCH], start=True, stop=False)
                                pe.wait_ge(w_done, hp * NI + (n + 1))
                                pe.matmul(yp[:, tc, lo:], vz[:, sbk, h, :], wgt[:, n % NW, lo:],
                                          start=False, stop=n == closes[tc]).then_inc(pv_done, 1)

                @block.scalar
                def _(act):
                    act.sem_inc(y_stored, TC)
                    act.preload_act_table_set("natural_log_exp_and_others")
                    with act.Fori(0, PAIRS) as hp:
                        for i in range(NI + 4):
                            if i < NI:
                                lo = items[i][2]
                                s_ = spl[:, i % NSP, lo:]
                                act.wait_ge(z_neg, hp * NI + (i + 1))
                                act.activation(s_, s_, ACT.Exp).then_inc(e_done, 1)
                                act.wait_ge(e_done, hp * NI + (i + 1))
                                act.activation(s_, s_, ACT.Ln, bias=1.0).then_inc(l_done, 1)
                            if 2 <= i < NI + 2:
                                n = i - 2
                                w_ = wgt[:, n % NW, items[n][2]:]
                                act.wait_ge(arg_done, hp * NI + (n + 1))
                                act.activation(w_, w_, ACT.Exp).then_inc(w_done, 1)
                            for tc in range(TC):
                                if i - 4 == closes[tc]:
                                    rwait(act, pv_done, hp * NI + (closes[tc] + 2))
                                    act.activation(featT[:, ds(hp * T + (T_SBQ * T + tc * NCH), NCH)], yp[:, tc, :],
                                                   ACT.Copy).then_inc(y_stored, 1)

                @block.vector
                def _(dve):
                    dve.wait_ge(masks_set, N_MASKS)
                    with dve.Fori(0, PAIRS) as hp:
                        rwait(dve, pv_done, hp * NI + 1)
                        dve.tensor_copy(ks[:, :], featT[:, ds(hp * T + T_SBK * T, T)]).then_inc(in_copied, 1)
                        for h in range(2):
                            dve.tensor_scalar(qz[:, h, :], featT[:, ds(hp * T + T_SBQ * T, T)],
                                              vec[:, V_HEADMASK + h:V_HEADMASK + h + 1], None, ALU.mult).then_inc(in_copied, 1)
                            dve.tensor_copy(vz[:, :, h, h * SB_DIM:(h + 1) * SB_DIM],
                                            vtok[:, :].rearrange("p (t c) -> p t c", t=TT)[:, :, ds(hp * P + h * SB_DIM, SB_DIM)]
                                            ).then_inc(in_copied, 1)
                        for i in range(NI + 3):
                            if i < NI:
                                tc, sbk, lo, h = items[i]
                                dve.wait_ge(z_done, hp * NI + (i + 1))
                                if i >= 3:
                                    dve.wait_ge(arg_done, hp * NI + (i - 2))
                                if tc * QB <= sbk:
                                    ins = dve.tensor_tensor(zsb[:, i % NZ, lo:], zp[:, i % 2, lo:], maskw[:, 0:NCH - lo], ALU.add)
                                else:
                                    ins = dve.tensor_copy(zsb[:, i % NZ, lo:], zp[:, i % 2, lo:])
                                ins.then_inc(z_copied, 1)
                                dve.wait_ge(z_copied, hp * NI + (i + 1))
                                if i >= NSP:
                                    dve.wait_ge(r_done, hp * NI + (i - NSP + 1))
                                    if items[i - NSP][1] > 0:
                                        dve.wait_ge(acc_done, hp * NA + n_acc[i - NSP])
                                dve.scalar_tensor_tensor(spl[:, i % NSP, lo:], zsb[:, i % NZ, lo:], -1.0, zsb[:, i % NZ, lo:],
                                                         ALU.mult, ALU.min).then_inc(z_neg, 1)
                            if 1 <= i < NI + 1:
                                n = i - 1
                                lo = items[n][2]
                                dve.wait_ge(l_done, hp * NI + (n + 1))
                                dve.scalar_tensor_tensor(spl[:, n % NSP, lo:], zsb[:, n % NZ, lo:], 0.0, spl[:, n % NSP, lo:],
                                                         ALU.max, ALU.add).then_inc(sp_done, 1)
                            if 2 <= i < NI + 2:
                                n = i - 2
                                lo = items[n][2]
                                dve.wait_ge(r_done, hp * NI + (n + 1))
                                if n >= NW:
                                    dve.wait_ge(pv_done, hp * NI + (n - NW + 2))
                                dve.tensor_tensor(wgt[:, n % NW, lo:], zsb[:, n % NZ, lo:], rp[:, n % 2, lo:],
                                                  ALU.subtract).then_inc(arg_done, 1)

        MB0 = T_SBK * T
        KSCALE = float(ML_DIM) ** -0.5
        with tensors() as st:
            acol = sb(st, "acol", [P, ML_HEADS, TT])
            with tensors() as st2:
                rlog = sb(st2, "rlog", [ML_HEADS, T])
                rsum = sb(st2, "rsum", [ML_HEADS, T])
                rmax = sb(st2, "rmax", [ML_HEADS, T])
                rone = sb(st2, "rone", [ML_HEADS, T])
                sel = sb(st2, "sel", [ML_HEADS, ML_HEADS, P])
                ident4 = sb(st2, "ident4", [ML_HEADS, ML_HEADS])
                ap_ = ps(st2, "ap", [P, TT, ML_HEADS])
                bp = ps(st2, "bp", [P, 4, NCH])
                sel_set, row_step = sem("sel_set"), sem("row_step")
                neg_ready, lnf_e, lnf_ready = sem("neg_ready"), sem("lnf_e"), sem("lnf_ready")
                a_ready, acol_done, acol_stored = sem("a_ready"), sem("acol_done"), sem("acol_stored")
                m_ready, bc_done, bc_stored = sem("m_ready"), sem("bc_done"), sem("bc_stored")
                irow, frow = ifrow[:, 0, :], ifrow[:, 1, :]
                bcasts = [(h, c, q) for h in range(ML_HEADS) for c in range(TC) for q in range(2)]

                with nc.Block() as block:

                    @block.gpsimd
                    def _(pool):
                        pool.memset(sel[:, :, :], 1.0).then_inc(sel_set, 1)
                        pool.memset(ident4[:, :], 1.0).then_inc(sel_set, 1)
                        pool.wait_ge(sel_set, 2)
                        pool.affine_select(out=sel[:, :, :], in_=sel[:, :, :], compare_op=ALU.is_equal, fill=0.0, base=0,
                                           pattern=[[-1, ML_HEADS], [0, P]], channel_multiplier=1).then_inc(sel_set, 1)
                        pool.affine_select(out=ident4[:, :], in_=ident4[:, :], compare_op=ALU.is_equal, fill=0.0, base=0,
                                           pattern=[[-1, ML_HEADS]], channel_multiplier=1).then_inc(sel_set, 1)

                    @block.vector
                    def _(dve):
                        dve.memset(rone[:, :], 1.0).then_inc(row_step, 1)
                        dve.scalar_tensor_tensor(rlog[:, :], frow, -1.0, frow, ALU.mult, ALU.min).then_inc(neg_ready, 1)
                        dve.wait_ge(lnf_ready, 1)
                        dve.scalar_tensor_tensor(rlog[:, :], frow, 0.0, rlog[:, :], ALU.min, ALU.subtract).then_inc(row_step, 1)
                        dve.wait_ge(row_step, 2)
                        dve.tensor_tensor_scan(rsum[:, :], rone[:, :], rlog[:, :], 0.0, ALU.mult, ALU.add).then_inc(row_step, 1)
                        dve.wait_ge(row_step, 3)
                        dve.tensor_tensor(irow, irow, rsum[:, :], ALU.subtract).then_inc(a_ready, 1)
                        dve.wait_ge(a_ready, 1)
                        dve.tensor_tensor_scan(rmax[:, :], irow, irow, 0.0, ALU.max, ALU.max).then_inc(row_step, 1)
                        dve.wait_ge(row_step, 4)
                        dve.tensor_tensor(rsum[:, :], rsum[:, :], rmax[:, :], ALU.add).then_inc(m_ready, 1)
                        dve.wait_ge(acol_done, 1)
                        dve.tensor_copy(acol[:, :, :], ap_[:, :, :].rearrange("p t h -> p h t")).then_inc(acol_stored, 1)

                    @block.scalar
                    def _(act):
                        act.preload_act_table_set("natural_log_exp_and_others")
                        act.wait_ge(neg_ready, 1)
                        act.activation(rlog[:, :], rlog[:, :], ACT.Exp).then_inc(lnf_e, 1)
                        act.wait_ge(lnf_e, 1)
                        act.activation(rlog[:, :], rlog[:, :], ACT.Ln, bias=1.0).then_inc(lnf_ready, 1)
                        for n, (h, c, q) in enumerate(bcasts):
                            act.wait_ge(bc_done, n + 1)
                            if q == 0:
                                act.activation(featT[:, MB0 + h * T + c * NCH:MB0 + h * T + (c + 1) * NCH], bp[:, n % 4, :],
                                               ACT.Copy).then_inc(bc_stored, 1)
                            else:
                                at = (h * TC + c) * 2 * NCH
                                act.activation(vtok[:, at:at + NCH], bp[:, n % 4, :], ACT.Exp, scale=-1.0).then_inc(bc_stored, 1)

                    @block.tensor
                    def _(pe):
                        pe.wait_ge(sel_set, 4)
                        pe.wait_ge(a_ready, 1)
                        for t in range(TT):
                            last = pe.matmul(ap_[:, t, :], irow[:, t * P:(t + 1) * P], ident4[:, :], start=True, stop=True)
                        last.then_inc(acol_done, 1)
                        pe.wait_ge(m_ready, 1)
                        for n, (h, c, q) in enumerate(bcasts):
                            if n >= 4:
                                pe.wait_ge(bc_stored, n - 3)
                            row = (rmax, rsum)[q]
                            pe.matmul(bp[:, n % 4, :], sel[:, h, :], row[:, c * NCH:(c + 1) * NCH], start=True, stop=True).then_inc(bc_done, 1)

            with tensors() as st2:
                NE = 3
                km = sb(st2, "km", [P, T])
                qm = sb(st2, "qm", [P, T])
                vm = sb(st2, "vm", [P, TT, P])
                ah = sb(st2, "ah", [P, TT])
                maskm = sb(st2, "maskm", [P, NCH])
                ex = sb(st2, "ex", [P, NE, NCH])
                sw = sb(st2, "sw", [P, NE, NCH])
                fin = sb(st2, "fin", [P, NCH])
                sp_ = ps(st2, "sps", [P, 2, NCH])
                num = ps(st2, "num", [P, TC, NCH])
                den = ps(st2, "den", [P, TC, NCH])
                items = causal_tiles()
                NI = len(items)
                closes = {tc: max(n for n in range(NI) if items[n][0] == tc) for tc in range(TC)}
                QB = NCH // P
                maskm_set, min_copied, mx_done, me_done = sem("maskm_set"), sem("min_copied"), sem("mx_done"), sem("me_done")
                s_done, sw_done, nd_done = sem("s_done"), sem("sw_done"), sem("nd_done")
                den_abs, fin_step, hout_done = sem("den_abs"), sem("fin_step"), sem("hout_done")
                N_COPY = 4

                with nc.Block() as block:

                    @block.gpsimd
                    def _(pool):
                        pool.memset(maskm[:, :], 0.0).then_inc(maskm_set, 1)
                        pool.wait_ge(maskm_set, 1)
                        pool.affine_select(out=maskm[:, 0:P], in_=maskm[:, 0:P], compare_op=ALU.is_ge, fill=BIG, base=0,
                                           pattern=[[1, P]], channel_multiplier=-1).then_inc(maskm_set, 1)

                    @block.tensor
                    def _(pe):
                        pe.sem_inc(nd_done, 1)
                        with pe.Fori(0, ML_HEADS) as h:
                            pe.wait_ge(min_copied, h * N_COPY + N_COPY)
                            for i in range(NI + 2):
                                if i < NI:
                                    tc, sbk, lo = items[i]
                                    if i >= 2:
                                        pe.wait_ge(sw_done, h * NI + (i - 1))
                                    pe.matmul(sp_[:, i % 2, lo:], km[:, sbk * P:(sbk + 1) * P],
                                              qm[:, tc * NCH + lo:(tc + 1) * NCH], start=True, stop=True).then_inc(s_done, 1)
                                if i >= 2:
                                    n = i - 2
                                    tc, sbk, lo = items[n]
                                    if sbk == 0:
                                        pe.wait_ge(hout_done, h * TC + (tc + 1))
                                    pe.wait_ge(sw_done, h * NI + (n + 1))
                                    w_ = sw[:, n % NE, lo:]
                                    pe.matmul(num[:, tc, lo:], vm[:, sbk, :], w_, start=sbk == 0, stop=n == closes[tc])
                                    pe.matmul(den[:, tc, lo:], ones[:, :], w_, start=sbk == 0, stop=n == closes[tc]).then_inc(nd_done, 1)

                    @block.scalar
                    def _(act):
                        with act.Fori(0, ML_HEADS) as h:
                            for i in range(NI + 3):
                                if i < NI:
                                    lo = items[i][2]
                                    act.wait_ge(mx_done, h * NI + (i + 1))
                                    act.activation(ex[:, i % NE, lo:], ex[:, i % NE, lo:], ACT.Exp, scale=-1.0).then_inc(me_done, 1)
                                for tc in range(TC):
                                    if i - 2 == closes[tc]:
                                        act.wait_ge(hout_done, h * TC + (tc + TC))
                                        act.wait_ge(nd_done, h * NI + (closes[tc] + 2))
                                        act.activation(fin[:, :], den[:, tc, :], ACT.Abs).then_inc(den_abs, 1)

                    @block.vector
                    def _(dve):
                        dve.sem_inc(hout_done, TC)
                        dve.wait_ge(maskm_set, 2)
                        with dve.Fori(0, ML_HEADS) as h:
                            rwait(dve, nd_done, h * NI + 1)
                            dve.tensor_copy(km[:, :], featT[:, ds(h * T + T_MLK * T, T)]).then_inc(min_copied, 1)
                            dve.tensor_copy(qm[:, :], featT[:, ds(h * T + T_MLQ * T, T)]).then_inc(min_copied, 1)
                            dve.tensor_copy(vm[:, :, :], vtok[:, :].rearrange("p (t c) -> p t c", t=TT)[:, :, ds(h * P + NCH, P)]
                                            ).then_inc(min_copied, 1)
                            dve.tensor_copy(ah[:, :], acol[:, :, :].rearrange("p h t -> p (h t)")[:, ds(h * TT, TT)]
                                            ).then_inc(min_copied, 1)
                            dve.wait_ge(min_copied, h * N_COPY + N_COPY)
                            for i in range(NI + 4):
                                if i < NI:
                                    tc, sbk, lo = items[i]
                                    m_ = featT[:, ds(h * T + (MB0 + tc * NCH + lo), NCH - lo)]
                                    if i >= NE:
                                        rwait(dve, sw_done, h * NI + (i - NE + 1))
                                    if tc * QB <= sbk:
                                        ins = dve.scalar_tensor_tensor(ex[:, i % NE, lo:], m_, ah[:, sbk:sbk + 1],
                                                                       maskm[:, 0:NCH - lo], ALU.subtract, ALU.max)
                                    else:
                                        ins = dve.tensor_scalar(ex[:, i % NE, lo:], m_, ah[:, sbk:sbk + 1], 0.0,
                                                                ALU.subtract, ALU.max)
                                    ins.then_inc(mx_done, 1)
                                if 1 <= i < NI + 1:
                                    n = i - 1
                                    lo = items[n][2]
                                    dve.wait_ge(s_done, h * NI + (n + 1))
                                    dve.wait_ge(me_done, h * NI + (n + 1))
                                    if n >= NE:
                                        dve.wait_ge(nd_done, h * NI + (n - NE + 2))
                                    dve.scalar_tensor_tensor(sw[:, n % NE, lo:], sp_[:, n % 2, lo:], KSCALE, ex[:, n % NE, lo:],
                                                             ALU.mult, ALU.mult).then_inc(sw_done, 1)
                                for tc in range(TC):
                                    if i - 3 == closes[tc]:
                                        rwait(dve, den_abs, h * TC + (tc + 1))
                                        dve.tensor_tensor(fin[:, :], fin[:, :], vtok[:, ds(h * (TC * 2 * NCH) + tc * 2 * NCH, NCH)],
                                                          ALU.max).then_inc(fin_step, 1)
                                        dve.wait_ge(fin_step, h * (2 * TC) + (2 * tc + 1))
                                        dve.reciprocal(fin[:, :], fin[:, :]).then_inc(fin_step, 1)
                                        rwait(dve, fin_step, h * (2 * TC) + (2 * tc + 2))
                                        dve.tensor_tensor(featT[:, ds(h * T + (T_MLQ * T + tc * NCH), NCH)], num[:, tc, :],
                                                          fin[:, :], ALU.mult).then_inc(hout_done, 1)

            with tensors() as st2:
                hsq = sb(st2, "hsq", [P, 2, T])
                hstd = sb(st2, "hstd", [P, 2, T])
                hs = ps(st2, "hs", [P, 2, TC, NCH])
                osig_done, hsq_done, hs_done, hstd_done = sem("osig_done"), sem("hsq_done"), sem("hs_done"), sem("hstd_done")
                hrec_done, hnorm_done, yml_done = sem("hrec_done"), sem("hnorm_done"), sem("yml_done")

                def tile(k):
                    return featT[:, k * T:(k + 1) * T]

                with nc.Block() as block:

                    @block.scalar
                    def _(act):
                        for h in range(ML_HEADS):
                            act.activation(tile(T_MLO + h), tile(T_MLO + h), ACT.Sigmoid).then_inc(osig_done, 1)
                        for h in range(ML_HEADS):
                            if h >= 2:
                                act.wait_ge(hs_done, h - 1)
                            act.activation(hsq[:, h % 2, :], tile(T_MLQ + h), ACT.Square).then_inc(hsq_done, 1)
                            act.wait_ge(hs_done, h + 1)
                            if h >= 2:
                                act.wait_ge(hnorm_done, h - 1)
                            act.activation(hstd[:, h % 2, :], hs[:, h % 2, :, :].rearrange("p c n -> p (c n)"), ACT.Sqrt,
                                           scale=1.0 / ML_DIM, bias=eps[:, 0:1]).then_inc(hstd_done, 1)

                    @block.tensor
                    def _(pe):
                        for h in range(ML_HEADS):
                            pe.wait_ge(hsq_done, h + 1)
                            if h >= 2:
                                pe.wait_ge(hstd_done, h - 1)
                            for c in range(TC):
                                last = pe.matmul(hs[:, h % 2, c, :], ones[:, :], hsq[:, h % 2, c * NCH:(c + 1) * NCH],
                                                 start=True, stop=True)
                            last.then_inc(hs_done, 1)

                    @block.vector
                    def _(dve):
                        for h in range(ML_HEADS):
                            dve.wait_ge(hstd_done, h + 1)
                            dve.reciprocal(hstd[:, h % 2, :], hstd[:, h % 2, :]).then_inc(hrec_done, 1)
                            dve.wait_ge(hrec_done, h + 1)
                            dve.scalar_tensor_tensor(tile(T_MLQ + h), tile(T_MLQ + h), vec[:, V_MLNORM + h:V_MLNORM + h + 1],
                                                     hstd[:, h % 2, :], ALU.mult, ALU.mult).then_inc(hnorm_done, 1)
                            dve.wait_ge(hnorm_done, h + 1)
                            dve.wait_ge(osig_done, h + 1)
                            dve.tensor_tensor(tile(T_MLQ + h), tile(T_MLQ + h), tile(T_MLO + h), ALU.mult).then_inc(yml_done, 1)
        proj_st.close()

        merged_dram = nc.dram_tensor("merged_scratch", (KD, P, T), F32)
        with tensors() as st:
            NB = SB_HEADS * SB_DIM // P
            NWM = 2 * KD + 2 * NB
            wm = sb(st, "wm", [P, 2, NWM * P])
            sg = sb(st, "sg", [P, TC, 2, NCH])
            br = sb(st, "br", [P, TC, 2, NCH])
            mg = sb(st, "mg", [P, 2, T])
            mp = ps(st, "mp", [P, TC, 4, NCH])
            wm_loaded = [sem(f"wm_loaded{u}") for u in range(2)]
            mg_stored = [sem(f"mg_stored{u}") for u in range(2)]
            mm_done, sg_done, br_done, mg_done = sem("mm_done"), sem("sg_done"), sem("br_done"), sem("mg_done")
            mg_free = sem("mg_free")

            with nc.Block() as block:

                @block.sync
                def _(sp):
                    for u in range(2):
                        sp.dma_start(wm[:, u, :], w_merge[u]).then_inc(wm_loaded[u], 16)

                    def store(j, u, reload):
                        sp.wait_ge(mg_done, j * (2 * TC) + (TC * u + 2 * TC))
                        sp.dma_start(merged_dram[:, :, :].rearrange("n p t -> p n t")[:, ds(j * 2 + u, 1), :],
                                     mg[:, u:u + 1, :]).then_inc(mg_stored[u], 16)
                        if reload:
                            sp.dma_start(wm[:, u:u + 1, :], w_merge.rearrange("n p c -> p n c")[:, ds(j * 2 + (u + 2), 1), :]
                                         ).then_inc(wm_loaded[u], 16)
                        sp.wait_ge(mg_stored[u], j * 16 + 16)
                        sp.sem_inc(mg_free, 1)

                    with sp.Fori(0, KD // 2 - 1) as j:
                        for u in range(2):
                            store(j, u, True)
                    for u in range(2):
                        store(KD // 2 - 1, u, False)

                @block.tensor
                def _(pe):
                    with pe.Fori(0, KD // 2) as j:
                        for u in range(2):
                            pe.wait_ge(wm_loaded[u], j * 16 + 16)
                            for c in range(TC):
                                pe.wait_ge(mg_done, j * 4 + (2 * u + c + 1))
                                at = 0
                                for q, (base, n) in enumerate(((None, KD), (None, KD), (T_SBQ, NB), (T_MLQ, NB))):
                                    for k in range(n):
                                        src = xnT if base is None else featT
                                        col = ((base or 0) + k) * T + c * NCH
                                        last = pe.matmul(mp[:, c, q, :], wm[:, u, (at + k) * P:(at + k + 1) * P],
                                                         src[:, col:col + NCH], start=k == 0, stop=k == n - 1)
                                    at += n
                                last.then_inc(mm_done, 1)

                @block.scalar
                def _(act):
                    with act.Fori(0, KD // 2) as j:
                        for u in range(2):
                            for c in range(TC):
                                act.wait_ge(mm_done, j * 4 + (2 * u + c + 1))
                                act.activation(sg[:, c, :, :], mp[:, c, 0:2, :], ACT.Sigmoid).then_inc(sg_done, 1)

                @block.vector
                def _(dve):
                    dve.sem_inc(mg_done, TC)
                    dve.sem_inc(mg_free, 2)
                    with dve.Fori(0, KD // 2) as j:
                        for u in range(2):
                            for c in range(TC):
                                dve.wait_ge(sg_done, j * 4 + (2 * u + c + 1))
                                dve.tensor_tensor(br[:, c, :, :], sg[:, c, :, :], mp[:, c, 2:4, :], ALU.mult).then_inc(br_done, 1)
                                dve.wait_ge(br_done, j * 4 + (2 * u + c + 1))
                                if c == 0:
                                    dve.wait_ge(mg_free, j * 2 + (u + 1))
                                dve.tensor_tensor(mg[:, u, c * NCH:(c + 1) * NCH], br[:, c, 0, :], br[:, c, 1, :],
                                                  ALU.add).then_inc(mg_done, 1)
        mix_st.close()

        e_idx = sb(ctx, "e_idx", [P, TT * NSEL], I32)
        gate = sb(ctx, "gate", [P, TT * NSEL])
        with tensors() as st:
            wo = sb(st, "wo", [P, KD, D])
            wq = sb(st, "wq", [P, KD, QT * P])
            kT = sb(st, "kT", [P, QT, P])
            nrow = sb(st, "nrow", [P, D])
            mst = sb(st, "mst", [P, KD, P])
            xt = sb(st, "xt", [P, D])
            ht = sb(st, "ht", [P, D])
            hnt = sb(st, "hnt", [P, D])
            hnT = sb(st, "hnT", [P, KD, P])
            qT = sb(st, "qT", [P, QT, P])
            sc = sb(st, "sc", [P, QT, NKEYS])
            cand = sb(st, "cand", [P, PH, TOPK * TOPK])
            eq = sb(st, "eq", [P, NSEL, TOPK])
            v16 = sb(st, "v16", [P, PH, 2, TOPK])
            i16 = sb(st, "i16", [P, PH, 2, TOPK], U32)
            i16f = sb(st, "i16f", [P, PH, 2, TOPK])
            top = sb(st, "top", [P, PH, TOPK])
            topi = sb(st, "topi", [P, PH, TOPK], U32)
            ab = sb(st, "ab", [P, 2, NSEL], U32)
            abf = sb(st, "abf", [P, 2, NSEL])
            esel = sb(st, "esel", [P, 2, NSEL])
            gsum = sb(st, "gsum", [P, PH])
            io16 = sb(st, "io16", [P, TOPK])
            ident = sb(st, "ident", [P, P])
            ss = sb(st, "ss", [P, 2])
            rs = sb(st, "rs", [P, 1])
            xp = ps(st, "xp", [P, D])
            tp = ps(st, "tp", [P, D])
            qp = ps(st, "qp", [P, 4, NCH])
            w6_loaded = [sem(f"w6_loaded{n}") for n in range(4)]
            m_loaded, xt_loaded = sem("m_loaded"), sem("xt_loaded")
            ident_set, mix_done, h_ready, ss_ready, std6_ready = (sem(n) for n in (
                "ident_set", "mix_done", "h_ready", "ss_ready", "std6_ready"))
            rstd6_ready, hn_ready, tp_done, hnT_ready = (sem(n) for n in ("rstd6_ready", "hn_ready", "tp_done", "hnT_ready"))
            q_done, qT_ready, sc_done, sc_stored = (sem(n) for n in ("q_done", "qT_ready", "sc_done", "sc_stored"))
            k_step, sc_read, row_free = (sem(n) for n in ("k_step", "sc_read", "row_free"))
            K_STEPS = 16
            h_stored, hn_stored = sem("h_stored"), sem("hn_stored")
            NG = 4
            GH = QT // NG

            with nc.Block() as block:

                @block.sync
                def _(sp):
                    sp.dma_start(wo[:, :, :], w_out).then_inc(w6_loaded[0], 16)
                    mv = merged_dram[:, :, :].rearrange("k p t -> p k t")

                    def load_tile(i):
                        sp.dma_start(mst[:, :, :], mv[:, :, ds(i * P, P)]).then_inc(m_loaded, 16)
                        sp.dma_start(xt[:, :], x[ds(i * P, P), :]).then_inc(xt_loaded, 16)

                    def store_tile(i):
                        sp.wait_ge(h_ready, i + 2)
                        sp.dma_start(h_dram[ds(i * P, P), :], ht[:, :]).then_inc(h_stored, 16)
                        sp.wait_ge(hn_ready, i + 1)
                        sp.dma_start(hn_dram[ds(i * P, P), :], hnt[:, :]).then_inc(hn_stored, 16)
                        sp.wait_ge(h_stored, i * 16 + 16)
                        sp.wait_ge(hn_stored, i * 16 + 16)
                        sp.sem_inc(row_free, 1)

                    load_tile(0)
                    sp.dma_start(nrow[:, :], rows[0:1, :].broadcast_to([P, D])).then_inc(w6_loaded[3], 16)
                    sp.dma_start(wq[:, :, :], w_query).then_inc(w6_loaded[1], 16)
                    sp.dma_start(kT[:, :, :], keysT).then_inc(w6_loaded[2], 16)
                    with sp.Fori(0, TT - 1) as i:
                        sp.wait_ge(h_ready, i + 2)
                        load_tile(i + 1)
                        store_tile(i)
                    store_tile(TT - 1)

                @block.gpsimd
                def _(pool):
                    pool.iota(io16[:, :], pattern=[[1, TOPK]], base=0, channel_multiplier=0,
                              allow_small_or_imprecise_dtypes=True)
                    pool.memset(ident[:, :], 1.0).then_inc(ident_set, 1)
                    pool.wait_ge(ident_set, 1)
                    pool.affine_select(out=ident[:, :], in_=ident[:, :], compare_op=ALU.is_equal, fill=0.0, base=0,
                                       pattern=[[-1, P]], channel_multiplier=1).then_inc(ident_set, 1)

                @block.tensor
                def _(pe):
                    for n in range(3):
                        pe.wait_ge(w6_loaded[n], 16)
                    pe.wait_ge(ident_set, 2)
                    with pe.Fori(0, TT) as i:
                        pe.wait_ge(m_loaded, i * 16 + 16)
                        pe.wait_ge(h_ready, i + 1)
                        for c in range(D // NCH):
                            for k in range(KD):
                                last = pe.matmul(xp[:, c * NCH:(c + 1) * NCH], mst[:, k, :], wo[:, k, c * NCH:(c + 1) * NCH],
                                                 start=k == 0, stop=k == KD - 1)
                        last.then_inc(mix_done, 1)
                        pe.wait_ge(hn_ready, i + 1)
                        for k in range(KD):
                            last = pe.transpose(tp[:, k * P:(k + 1) * P], hnt[:, k * P:(k + 1) * P], ident[:, :])
                        last.then_inc(tp_done, 1)
                        pe.wait_ge(hnT_ready, i + 1)
                        for g in range(NG):
                            pe.wait_ge(sc_stored, i * NG + (g + 1))
                            for c in range(GH):
                                for k in range(KD):
                                    last = pe.matmul(qp[:, g, c * P:(c + 1) * P], wq[:, k, (g * GH + c) * P:(g * GH + c + 1) * P],
                                                     hnT[:, k, :], start=k == 0, stop=k == KD - 1)
                            last.then_inc(q_done, 1)
                        for g in range(NG):
                            pe.wait_ge(qT_ready, i * NG + (g + 1))
                            for c in range(GH):
                                last = pe.matmul(qp[:, g, c * P:(c + 1) * P], qT[:, g * GH + c, :], kT[:, g * GH + c, :],
                                                 start=True, stop=True)
                            last.then_inc(sc_done, 1)

                @block.scalar
                def _(act):
                    act.sem_inc(sc_stored, NG)
                    with act.Fori(0, TT) as i:
                        act.wait_ge(h_ready, i + 2)
                        act.activation(hnt[:, :], ht[:, :], ACT.Square, accum_out=ss[:, 0:1]).then_inc(ss_ready, 1)
                        act.wait_ge(ss_ready, i + 1)
                        act.activation(ss[:, 1:2], ss[:, 0:1], ACT.Sqrt, scale=1.0 / D, bias=eps[:, 0:1]).then_inc(std6_ready, 1)
                        act.wait_ge(tp_done, i + 1)
                        act.activation(hnT[:, :, :].rearrange("p k t -> p (k t)"), tp[:, :], ACT.Copy).then_inc(hnT_ready, 1)
                        for g in range(NG):
                            act.wait_ge(q_done, i * NG + (g + 1))
                            act.activation(qT[:, g * GH:(g + 1) * GH, :].rearrange("p c t -> p (c t)"), qp[:, g, :],
                                           ACT.Copy).then_inc(qT_ready, 1)
                        act.wait_ge(sc_read, i + 1)
                        for g in range(NG):
                            act.wait_ge(sc_done, i * NG + (g + 1))
                            act.activation(sc[:, g * GH:(g + 1) * GH, :].rearrange("p c t -> p (c t)"), qp[:, g, :],
                                           ACT.Copy).then_inc(sc_stored, 1)

                @block.vector
                def _(dve):
                    dve.sem_inc(h_ready, 1)
                    dve.sem_inc(row_free, 1)
                    dve.sem_inc(sc_read, 1)
                    steps = [0]

                    def mark(ins):
                        ins.then_inc(k_step, 1)
                        steps[0] += 1

                    def after_marks(i):
                        rwait(dve, k_step, i * K_STEPS + steps[0])

                    def norm(i):
                        rwait(dve, row_free, i + 1)
                        rwait(dve, xt_loaded, i * 16 + 16)
                        rwait(dve, mix_done, i + 1)
                        dve.tensor_tensor(ht[:, :], xt[:, :], xp[:, :], ALU.add).then_inc(h_ready, 1)
                        rwait(dve, std6_ready, i + 1)
                        dve.reciprocal(rs[:, :], ss[:, 1:2]).then_inc(rstd6_ready, 1)
                        rwait(dve, rstd6_ready, i + 1)
                        dve.wait_ge(w6_loaded[3], 16)
                        dve.scalar_tensor_tensor(hnt[:, :], ht[:, :], rs[:, 0:1], nrow[:, :], ALU.mult, ALU.mult).then_inc(hn_ready, 1)

                    halves = [(h, f) for h in range(PH) for f in range(2)]

                    def top_of_halves(i):
                        steps[0] = 0
                        rwait(dve, sc_stored, i * NG + 2 * NG)
                        for h, f in halves:
                            last = dve.max(v16[:, h, f, 0:8], sc[:, 2 * h + f, :])
                        mark(last)
                        after_marks(i)
                        for h, f in halves:
                            dve.max_index(i16[:, h, f, 0:8], v16[:, h, f, 0:8], sc[:, 2 * h + f, :])
                            last = dve.match_replace(sc[:, 2 * h + f, :], v16[:, h, f, 0:8], sc[:, 2 * h + f, :], NEG)
                        mark(last)
                        after_marks(i)
                        for h, f in halves:
                            last = dve.max(v16[:, h, f, 8:16], sc[:, 2 * h + f, :])
                        mark(last)
                        after_marks(i)
                        for h, f in halves:
                            last = dve.max_index(i16[:, h, f, 8:16], v16[:, h, f, 8:16], sc[:, 2 * h + f, :])
                        last.then_inc(sc_read, 1)

                    def top_of_pairs(i):
                        rwait(dve, sc_read, i + 2)
                        dve.tensor_copy(i16f[:, :, :, :], i16[:, :, :, :])
                        mark(dve.tensor_tensor(
                            cand[:, :, :].rearrange("p h (a b) -> p h a b", a=TOPK),
                            v16[:, :, 0, :].unsqueeze(3).broadcast_to([P, PH, TOPK, TOPK]),
                            v16[:, :, 1, :].unsqueeze(2).broadcast_to([P, PH, TOPK, TOPK]), ALU.add))
                        after_marks(i)
                        for h in range(PH):
                            last = dve.max(top[:, h, 0:8], cand[:, h, :])
                        mark(last)
                        after_marks(i)
                        for h in range(PH):
                            dve.max_index(topi[:, h, 0:8], top[:, h, 0:8], cand[:, h, :])
                            last = dve.match_replace(cand[:, h, :], top[:, h, 0:8], cand[:, h, :], NEG)
                        mark(last)
                        after_marks(i)
                        for h in range(PH):
                            last = dve.max(top[:, h, 8:16], cand[:, h, :])
                        mark(last)
                        after_marks(i)
                        for h in range(PH):
                            last = dve.max_index(topi[:, h, 8:16], top[:, h, 8:16], cand[:, h, :])
                        mark(last)
                        after_marks(i)
                        ti = topi[:, :, :].rearrange("p h k -> p (h k)")
                        dve.tensor_scalar(ab[:, 0, :], ti, 4, None, ALU.logical_shift_right)
                        mark(dve.tensor_scalar(ab[:, 1, :], ti, TOPK - 1, None, ALU.bitwise_and))
                        after_marks(i)
                        mark(dve.tensor_copy(abf[:, :, :], ab[:, :, :]))
                        for f in range(2):
                            after_marks(i)
                            mark(dve.tensor_tensor(eq[:, :, :], abf[:, f, :].unsqueeze(2).broadcast_to([P, NSEL, TOPK]),
                                                   io16[:, :].unsqueeze(1).broadcast_to([P, NSEL, TOPK]), ALU.is_equal))
                            after_marks(i)
                            e4 = eq[:, :, :].rearrange("p (h k) a -> p h k a", h=PH)
                            mark(dve.tensor_tensor(e4, e4, i16f[:, :, f, :].unsqueeze(2).broadcast_to([P, PH, TOPK, TOPK]),
                                                   ALU.mult))
                            after_marks(i)
                            last = dve.tensor_reduce(esel[:, f, :], eq[:, :, :], AX.X, ALU.add)
                            mark(last)
                        after_marks(i)
                        dve.scalar_tensor_tensor(e_idx[:, ds(i * NSEL, NSEL)], esel[:, 0, :], float(NKEYS), esel[:, 1, :],
                                                 ALU.mult, ALU.add)
                        dve.tensor_tensor(gate[:, ds(i * NSEL, NSEL)].rearrange("p (h k) -> p h k", h=PH), top[:, :, :],
                                          top[:, :, 0:1].broadcast_to([P, PH, TOPK]), ALU.subtract)
                        assert steps[0] == K_STEPS

                    dve.wait_ge(ident_set, 1)
                    norm(0)
                    with dve.Fori(0, TT - 1) as i:
                        top_of_halves(i)
                        norm(i + 1)
                        top_of_pairs(i)
                    top_of_halves(TT - 1)
                    top_of_pairs(TT - 1)

        with tensors() as st:
            G, RING = 4, 4
            NGR = NSEL // G
            rowsb = sb(st, "rowsb", [P, RING, G, 2 * D])
            hrow = sb(st, "hrow", [P, D])
            hnrow = sb(st, "hnrow", [P, D])
            frow_ = sb(st, "frow", [P, D])
            acc7 = sb(st, "acc7", [P, D])
            junk2 = sb(st, "junk2", [P, D])
            idxg = sb(st, "idxg", [P, RING, G], I32)
            gmt = sb(st, "gmt", [P, RING, G])
            dots = sb(st, "dots", [P, RING, G])
            wg = sb(st, "wg", [P, RING, G])
            gs = sb(st, "gs", [P, TT * PH])
            ss7 = sb(st, "ss7", [P, 2])
            g_loaded = [[sem(f"g_loaded{r}_{k}") for k in range(G)] for r in range(RING)]
            t7_loaded, f7_loaded = [sem("h7_loaded"), sem("hn7_loaded")], sem("f7_loaded")
            gexp_done, gate_step = sem("gexp_done"), sem("gate_step")
            idx_ready, dot_done, gelu_done, wg_done, res_done = (sem(n) for n in (
                "idx_ready", "dot_done", "gelu_done", "wg_done", "res_done"))
            acc_step, y7_ready, ss7_ready, std7_ready, rs7_ready, o7_ready, o7_stored = (sem(n) for n in (
                "acc_step", "y7_ready", "ss7_ready", "std7_ready", "rs7_ready", "o7_ready", "o7_stored"))
            tile_free = sem("tile_free")

            with nc.Block() as block:

                @block.sync
                def _(sp):
                    sp.dma_start(frow_[:, :], rows[1:2, :].broadcast_to([P, D])).then_inc(f7_loaded, 16)
                    with sp.Fori(0, TT) as i:
                        sp.wait_ge(tile_free, i + 1)
                        sp.dma_start(hrow[:, :], h_dram[ds(i * P, P), :]).then_inc(t7_loaded[0], 16)
                        sp.dma_start(hnrow[:, :], hn_dram[ds(i * P, P), :]).then_inc(t7_loaded[1], 16)
                        sp.wait_ge(o7_ready, i + 1)
                        sp.dma_start(out[ds(i * P, P), :], acc7[:, :]).then_inc(o7_stored, 16)
                        sp.wait_ge(o7_stored, i * 16 + 16)
                        sp.sem_inc(tile_free, 1)

                @block.gpsimd
                def _(pool):
                    with pool.Fori(0, TT * NGR // RING) as j:
                        for r in range(RING):
                            rwait(pool, acc_step, j * (RING * G) + (r + 1) * G)
                            pool.tensor_copy(idxg[:, r, :], e_idx[:, ds(j * (RING * G) + r * G, G)]).then_inc(idx_ready, 1)
                            rwait(pool, idx_ready, j * RING + (r + 1))
                            for k in range(G):
                                pool.indirect_dma_start(rowsb[:, r, k, :], None, uv,
                                                        bass.IndirectOffsetOnAxis(ap=idxg[:, r, k:k + 1], axis=0)
                                                        ).then_inc(g_loaded[r][k], 16)

                @block.scalar
                def _(act):
                    act.activation(gate[:, :], gate[:, :], ACT.Exp).then_inc(gexp_done, 1)
                    with act.Fori(0, TT) as i:
                        with act.Fori(0, NGR // RING) as j:
                            for r in range(RING):
                                act.wait_ge(dot_done, i * NGR + j * RING + (r + 1))
                                act.activation(gmt[:, r, :], dots[:, r, :], ACT.Gelu).then_inc(gelu_done, 1)
                        act.wait_ge(y7_ready, i + 1)
                        act.activation(junk2[:, :], acc7[:, :], ACT.Square, accum_out=ss7[:, 0:1]).then_inc(ss7_ready, 1)
                        act.wait_ge(ss7_ready, i + 1)
                        act.activation(ss7[:, 1:2], ss7[:, 0:1], ACT.Sqrt, scale=1.0 / D, bias=eps[:, 0:1]).then_inc(std7_ready, 1)

                @block.vector
                def _(dve):
                    dve.sem_inc(tile_free, 1)
                    dve.sem_inc(acc_step, RING * G)
                    dve.wait_ge(gexp_done, 1)
                    g3 = gate[:, :].rearrange("p (n k) -> p n k", k=TOPK)
                    dve.tensor_reduce(gs[:, :], g3, AX.X, ALU.add).then_inc(gate_step, 1)
                    dve.wait_ge(gate_step, 1)
                    dve.reciprocal(gs[:, :], gs[:, :]).then_inc(gate_step, 1)
                    dve.wait_ge(gate_step, 2)
                    dve.tensor_tensor(g3, g3, gs[:, :].unsqueeze(2).broadcast_to([P, TT * PH, TOPK]), ALU.mult).then_inc(gate_step, 1)
                    dve.wait_ge(gate_step, 3)

                    def dot(i, j, r):
                        for k in range(G):
                            rwait(dve, g_loaded[r][k], i * (NGR // RING * 16) + j * 16 + 16)
                            ins = dve.tensor_tensor_reduce(rowsb[:, r, k, 0:D], rowsb[:, r, k, 0:D], hnrow[:, :], 1.0, 0.0,
                                                           ALU.mult, ALU.add, dots[:, r, k:k + 1])
                        ins.then_inc(dot_done, 1)

                    def weigh(i, j, r, n):
                        rwait(dve, gelu_done, n)
                        dve.tensor_tensor(wg[:, r, :], gmt[:, r, :], gate[:, ds(i * NSEL + j * (RING * G) + r * G, G)],
                                          ALU.mult).then_inc(wg_done, 1)
                        rwait(dve, wg_done, n)
                        for k in range(G):
                            rwait(dve, acc_step, (n - 1) * G + (k + RING * G))
                            ins = dve.scalar_tensor_tensor(acc7[:, :], rowsb[:, r, k, D:2 * D], wg[:, r, k:k + 1], acc7[:, :],
                                                           ALU.mult, ALU.add)
                            ins.then_inc(acc_step, 1)

                    with dve.Fori(0, TT) as i:
                        rwait(dve, t7_loaded[0], i * 16 + 16)
                        rwait(dve, t7_loaded[1], i * 16 + 16)
                        dve.tensor_copy(acc7[:, :], hrow[:, :]).then_inc(res_done, 1)
                        rwait(dve, res_done, i + 1)
                        with dve.Fori(0, NGR // RING) as j:
                            for r in range(RING):
                                dot(i, j, r)
                                weigh(i, j, r, i * NGR + j * RING + (r + 1))
                        rwait(dve, acc_step, i * NSEL + (NSEL + RING * G))
                        dve.sem_inc(y7_ready, 1)
                        rwait(dve, std7_ready, i + 1)
                        dve.reciprocal(ss7[:, 0:1], ss7[:, 1:2]).then_inc(rs7_ready, 1)
                        rwait(dve, rs7_ready, i + 1)
                        dve.wait_ge(f7_loaded, 16)
                        dve.scalar_tensor_tensor(acc7[:, :], acc7[:, :], ss7[:, 0:1], frow_[:, :], ALU.mult, ALU.mult).then_inc(o7_ready, 1)


def kernel(**inputs):
    import concourse.bacc as bacc
    from concourse.bass_utils import run_bass_kernel_spmd

    a = {k: np.asarray(v) for k, v in inputs.items()}
    c = np.ascontiguousarray

    def tiles(w, first, n):
        k = w.shape[0] // P
        return w[:, first:first + n * P].reshape(k, P, n, P).transpose(2, 1, 0, 3).reshape(n, P, k * P)

    w_in = a["w_in"][0]
    sbw, mlw = SB_HEADS * SB_DIM, ML_HEADS * ML_DIM
    o_ml = 3 * sbw
    o_v, o_o = o_ml + 2 * mlw, o_ml + 3 * mlw
    o_if = o_ml + 4 * mlw
    o_g = o_if + 2 * ML_HEADS
    x = a["x"].reshape(T, D)
    w_feat = np.concatenate([tiles(w_in, o_ml, 8), tiles(w_in, o_o, 4), tiles(w_in, 0, 4), tiles(w_in, sbw, 4)])
    w_if = w_in[:, o_if:o_g].reshape(KD, P, 2 * ML_HEADS).transpose(1, 0, 2)
    w_tok = np.concatenate([w_in[:, 2 * sbw:o_ml], w_in[:, o_v:o_o]], axis=1).reshape(KD, P, 2 * NCH).transpose(1, 0, 2)
    w_merge = np.concatenate([tiles(w_in, o_g, KD), tiles(w_in, o_g + D, KD),
                              tiles(a["w_branch_sb"][0], 0, KD), tiles(a["w_branch_ml"][0], 0, KD)], axis=2)
    w_out = a["w_out"][0].reshape(KD, P, D).transpose(1, 0, 2)
    w_query = a["peer_w_query"][0].reshape(KD, P, QT * P).transpose(1, 0, 2)
    keys = np.stack([a["peer_keys1"][0], a["peer_keys2"][0]], axis=1)
    keysT = keys.transpose(3, 0, 1, 2).reshape(P, QT, NKEYS)
    uv = np.concatenate([a["peer_u"][0], a["peer_v"][0]], axis=1)
    rows = np.stack([a["norm_ffn_w"][0], a["norm_final_w"]])

    vecs = np.zeros((P, N_VEC), np.float32)
    vecs[:, V_NORM1:V_NORM1 + KD] = a["norm_mix_w"][0].reshape(KD, P).T
    vecs[:, V_MLNORM:V_MLNORM + ML_HEADS] = a["mlstm_norm_w"][0].reshape(ML_HEADS, P).T
    vecs[:SB_DIM, V_HEADMASK] = SB_DIM ** -0.5
    vecs[SB_DIM:, V_HEADMASK + 1] = SB_DIM ** -0.5
    vecs[:ML_HEADS, V_BI] = a["b_igate"][0]
    vecs[:ML_HEADS, V_BF] = a["b_fgate"][0]
    cv = np.concatenate([a["conv_w"][0], a["conv_b"]], axis=0)
    vecs[:, V_CONV:] = cv.reshape(CONV + 1, N_CONV, P).transpose(2, 1, 0).reshape(P, N_CONV * (CONV + 1))

    arrays = {"xT": x.T, "x_rows": x, "vecs": vecs, "w_feat": w_feat, "w_if": w_if, "w_tok": w_tok, "w_merge": w_merge,
              "w_out_": w_out, "w_query_": w_query, "keysT": keysT, "uv": uv, "rows": rows}
    arrays = {k: c(v) for k, v in arrays.items()}
    nc = bacc.Bacc("TRN2", target_bir_lowering=False, num_devices=1)
    args = [nc.dram_tensor(n, v.shape, mybir.dt.from_np(v.dtype), kind="ExternalInput").ap() for n, v in arrays.items()]
    out = nc.dram_tensor("out", (T, D), F32, kind="ExternalOutput").ap()
    build(nc, *args, out)
    r = run_bass_kernel_spmd(nc, [arrays], core_ids=[0])
    return r.results[0]["out"].reshape(1, T, D)
```

```python
from contextlib import ExitStack

import numpy as np

import concourse.bass as bass
from concourse import mybir

F32 = mybir.dt.float32
I32 = mybir.dt.int32
U32 = mybir.dt.uint32
ALU = mybir.AluOpType
ACT = mybir.ActivationFunctionType
AX = mybir.AxisListType

P = 128
T = 1024
D = 1024
KD = D // P
TT = T // P
NCH = 512
TC = T // NCH
EPS = 1e-6

SB_HEADS, SB_DIM = 8, 64
PAIRS = SB_HEADS // 2
ML_HEADS, ML_DIM = 4, 128
CONV = 4

PH, NKEYS, TOPK = 8, 128, 16
NSEL = PH * TOPK
QT = 2 * PH

T_MLQ, T_MLK, T_MLO, T_SBQ, T_SBK, N_FEAT = 0, 4, 8, 12, 16, 20
N_CONV = 8

V_NORM1, V_MLNORM, V_HEADMASK, V_BI, V_BF, V_CONV = 0, 8, 12, 14, 15, 16
N_VEC = V_CONV + N_CONV * (CONV + 1)

NEG = -3.0e38
BIG = 1.0e30


def ds(start, size):
    return bass.ds(start, size)


def causal_tiles():
    return [
        (tc, sb, max(0, sb - tc * (NCH // P)) * P)
        for tc in range(TC)
        for sb in range((tc + 1) * (NCH // P))
    ]


def build(nc, xT, x, vecs, w_feat, w_if, w_tok, w_merge, w_out, w_query, keysT, uv, rows, out):
    ctx = ExitStack()
    with ctx:
        def sem(name):
            return ctx.enter_context(nc.semaphore(name))

        waits_passed = sem("waits_passed")

        def tensors():
            return ExitStack()

        def sb(st, name, shape, dt=F32):
            return st.enter_context(nc.sbuf_tensor(name, shape, dt))

        def ps(st, name, shape, dt=F32):
            return st.enter_context(nc.psum_tensor(name, shape, dt))

        def rwait(eng, s, value):
            eng.wait_ge(s, value)
            eng.sem_inc(waits_passed, 1)

        h_dram = nc.dram_tensor("h_scratch", (T, D), F32)
        hn_dram = nc.dram_tensor("hn_scratch", (T, D), F32)

        vec = sb(ctx, "vec", [P, N_VEC])
        ones = sb(ctx, "ones", [P, P])
        eps = sb(ctx, "eps", [P, 1])

        mix_st = ctx.enter_context(tensors())
        xnT = sb(mix_st, "xnT", [P, KD * T])
        featT = sb(mix_st, "featT", [P, N_FEAT * T])
        proj_st = ctx.enter_context(tensors())
        vtok = sb(proj_st, "vtok", [P, TT * 2 * NCH])
        ifrow = sb(proj_st, "ifrow", [ML_HEADS, 2, T])

        with tensors() as st:
            sq = sb(st, "sq", [P, 2, T])
            rstd = sb(st, "rstd", [P, T])
            ssum = ps(st, "ssum", [P, T])
            wt = featT[:, T_SBQ * T:N_FEAT * T].rearrange("p (k c) -> p k c", k=KD)
            wt_loaded = sem("wt_loaded")
            x_loaded = [sem(f"x_loaded{k}") for k in range(KD)]
            vec_loaded = sem("vec_loaded")
            ones_set = sem("ones_set")
            sq_ready = sem("sq_ready")
            sq_summed = sem("sq_summed")
            std_ready = sem("std_ready")
            rstd_ready = sem("rstd_ready")

            with nc.Block() as block:

                @block.sync
                def _(sp):
                    xv = xT.rearrange("(k p) t -> k p t", p=P)
                    for k in range(KD):
                        sp.dma_start(xnT[:, k * T:(k + 1) * T], xv[k]).then_inc(x_loaded[k], 16)
                    sp.dma_start(vec[:, :], vecs).then_inc(vec_loaded, 16)
                    sp.dma_start(wt, w_tok).then_inc(wt_loaded, 16)

                @block.gpsimd
                def _(pool):
                    pool.memset(eps[:, :], EPS)
                    pool.memset(ones[:, :], 1.0).then_inc(ones_set, 1)

                @block.scalar
                def _(act):
                    for k in range(KD):
                        act.wait_ge(x_loaded[k], 16)
                        if k >= 2:
                            act.wait_ge(sq_summed, k - 1)
                        act.activation(sq[:, k % 2, :], xnT[:, k * T:(k + 1) * T], ACT.Square).then_inc(sq_ready, 1)
                    act.wait_ge(sq_summed, KD)
                    act.wait_ge(ones_set, 1)
                    act.activation(rstd[:, :], ssum[:, :], ACT.Sqrt, scale=1.0 / D, bias=eps[:, 0:1]).then_inc(std_ready, 1)

                @block.tensor
                def _(pe):
                    pe.wait_ge(ones_set, 1)
                    for k in range(KD):
                        pe.wait_ge(sq_ready, k + 1)
                        for c in range(TC):
                            last = pe.matmul(ssum[:, c * NCH:(c + 1) * NCH], ones[:, :],
                                             sq[:, k % 2, c * NCH:(c + 1) * NCH], start=k == 0, stop=k == KD - 1)
                        last.then_inc(sq_summed, 1)

                @block.vector
                def _(dve):
                    dve.wait_ge(std_ready, 1)
                    dve.reciprocal(rstd[:, :], rstd[:, :]).then_inc(rstd_ready, 1)
                    dve.wait_ge(rstd_ready, 1)
                    dve.wait_ge(vec_loaded, 16)
                    for k in range(KD):
                        if k == 0:
                            for kk in range(KD):
                                dve.wait_ge(x_loaded[kk], 16)
                        xk = xnT[:, k * T:(k + 1) * T]
                        dve.scalar_tensor_tensor(xk, xk, vec[:, V_NORM1 + k:V_NORM1 + k + 1], rstd[:, :],
                                                 ALU.mult, ALU.mult).then_inc(rstd_ready, 1)

        with tensors() as st:
            wf = sb(st, "wf", [P, 2, KD * P])
            wif = sb(st, "wif", [P, KD, 2 * ML_HEADS])
            xs = sb(st, "xs", [P, 2, KD, P])
            conv = sb(st, "conv", [P, 2, T])
            pf = ps(st, "pf", [P, 2, TC, NCH])
            pif = ps(st, "pif", [P, 2, TC, NCH])
            wf_loaded = [sem(f"wf_loaded{u}") for u in range(2)]
            wif_loaded = sem("wif_loaded")
            feat_done = sem("feat_done")
            evac_act, evac_dve = sem("evac_act"), sem("evac_dve")
            if_done, if_ready = sem("if_done"), sem("if_ready")
            xs_ready, tok_done = sem("xs_ready"), sem("tok_done")
            tevac_act, tevac_dve = sem("tevac_act"), sem("tevac_dve")
            conv_step, silu_done = sem("conv_step"), sem("silu_done")
            NSTEP = CONV

            with nc.Block() as block:

                @block.sync
                def _(sp):
                    sp.dma_start(wif[:, :, :], w_if).then_inc(wif_loaded, 16)
                    for u in range(2):
                        sp.dma_start(wf[:, u, :], w_feat[u]).then_inc(wf_loaded[u], 16)
                    with sp.Fori(0, N_FEAT // 2 - 1) as j:
                        for u in range(2):
                            sp.wait_ge(feat_done, j * 2 + (u + 1))
                            sp.dma_start(wf[:, u:u + 1, :], w_feat.rearrange("n p c -> p n c")[:, ds(j * 2 + (u + 2), 1), :]).then_inc(wf_loaded[u], 16)

                @block.gpsimd
                def _(pool):
                    xv = xnT[:, :].rearrange("p (k t) -> p k t", k=KD)
                    for u in range(2):
                        pool.tensor_copy(xs[:, u, :, :], xv[:, :, u * P:(u + 1) * P]).then_inc(xs_ready, 1)
                    with pool.Fori(0, TT // 2 - 1) as j:
                        for u in range(2):
                            rwait(pool, tok_done, j * 2 + (u + 1))
                            pool.tensor_copy(xs[:, u, :, :], xv[:, :, ds(j * (2 * P) + (u + 2) * P, P)]).then_inc(xs_ready, 1)

                @block.tensor
                def _(pe):
                    pe.wait_ge(wt_loaded, 16)
                    with pe.Fori(0, TT // 2) as j:
                        for u in range(2):
                            pe.wait_ge(xs_ready, j * 2 + (u + 1))
                            pe.wait_ge(tevac_act, j * 2 + (u + 1))
                            pe.wait_ge(tevac_dve, j * 2 + (u + 1))
                            for n in range(2):
                                for k in range(KD):
                                    last = pe.matmul(pf[:, u, n, :], xs[:, u, k, :], wt[:, k, n * NCH:(n + 1) * NCH],
                                                     start=k == 0, stop=k == KD - 1)
                            last.then_inc(tok_done, 1)
                    pe.wait_ge(wif_loaded, 16)
                    for g in range(2):
                        for c in range(TC):
                            for k in range(KD):
                                last = pe.matmul(pif[0:ML_HEADS, g, c, :], wif[:, k, g * ML_HEADS:(g + 1) * ML_HEADS],
                                                 xnT[:, k * T + c * NCH:k * T + (c + 1) * NCH],
                                                 start=k == 0, stop=k == KD - 1)
                    last.then_inc(if_done, 1)
                    pe.wait_ge(tevac_act, TT + 2)
                    pe.wait_ge(tevac_dve, TT + 2)
                    with pe.Fori(0, N_FEAT // 2) as j:
                        for u in range(2):
                            pe.wait_ge(wf_loaded[u], j * 16 + 16)
                            pe.wait_ge(evac_act, j * 2 + (u + 1))
                            pe.wait_ge(evac_dve, j * 2 + (u + 1))
                            for c in range(TC):
                                for k in range(KD):
                                    last = pe.matmul(pf[:, u, c, :], wf[:, u, k * P:(k + 1) * P],
                                                     xnT[:, k * T + c * NCH:k * T + (c + 1) * NCH],
                                                     start=k == 0, stop=k == KD - 1)
                            last.then_inc(feat_done, 1)

                @block.scalar
                def _(act):
                    act.sem_inc(evac_act, 2)
                    act.sem_inc(tevac_act, 2)
                    with act.Fori(0, TT // 2) as j:
                        for u in range(2):
                            rwait(act, tok_done, j * 2 + (u + 1))
                            act.activation(vtok[:, ds(j * (4 * NCH) + u * 2 * NCH, NCH)], pf[:, u, 0, :], ACT.Copy).then_inc(tevac_act, 1)
                    act.wait_ge(if_done, 1)
                    for g in range(2):
                        act.activation(ifrow[:, g, :], pif[0:ML_HEADS, g, :, :].rearrange("p c n -> p (c n)"), ACT.Identity,
                                       bias=vec[0:ML_HEADS, V_BI + g:V_BI + g + 1]).then_inc(if_ready, 1)

                    def evacuate(j, u, tile0):
                        rwait(act, feat_done, j * 2 + (tile0 + u + 1))
                        act.activation(featT[:, ds(j * (2 * T) + (tile0 + u) * T, NCH)], pf[:, u, 0, :], ACT.Copy).then_inc(evac_act, 1)

                    with act.Fori(0, N_CONV // 2) as j:
                        for u in range(2):
                            evacuate(j, u, 0)
                    with act.Fori(0, N_CONV // 2) as j:
                        for u in range(2):
                            evacuate(j, u, N_CONV)
                            rwait(act, conv_step, j * (2 * NSTEP) + (u + 1) * NSTEP)
                            act.activation(featT[:, ds(j * (2 * T) + (T_MLQ + u) * T, T)], conv[:, u, :], ACT.Silu).then_inc(silu_done, 1)
                    with act.Fori(0, N_FEAT // 2 - N_CONV) as j:
                        for u in range(2):
                            evacuate(j, u, 2 * N_CONV)

                @block.vector
                def _(dve):
                    dve.sem_inc(evac_dve, 2)
                    dve.sem_inc(tevac_dve, 2)
                    dve.sem_inc(silu_done, 2)
                    with dve.Fori(0, TT // 2) as j:
                        for u in range(2):
                            rwait(dve, tok_done, j * 2 + (u + 1))
                            dve.tensor_copy(vtok[:, ds(j * (4 * NCH) + (u * 2 + 1) * NCH, NCH)], pf[:, u, 1, :]).then_inc(tevac_dve, 1)

                    def evacuate(j, u, tile0):
                        rwait(dve, feat_done, j * 2 + (tile0 + u + 1))
                        dve.tensor_copy(featT[:, ds(j * (2 * T) + (tile0 + u) * T + NCH, NCH)], pf[:, u, 1, :]).then_inc(evac_dve, 1)

                    with dve.Fori(0, N_CONV // 2) as j:
                        for u in range(2):
                            evacuate(j, u, 0)
                    dve.wait_ge(evac_dve, N_CONV + 2)
                    dve.wait_ge(evac_act, N_CONV + 2)
                    with dve.Fori(0, N_CONV // 2) as j:
                        for u in range(2):
                            evacuate(j, u, N_CONV)

                            def tap(n, j=j, u=u):
                                return vec[:, ds(j * (2 * (CONV + 1)) + (V_CONV + u * (CONV + 1) + n), 1)]

                            rwait(dve, silu_done, j * 2 + (u + 1))
                            dve.tensor_scalar(conv[:, u, :], featT[:, ds(j * (2 * T) + (T_MLQ + u) * T, T)],
                                              tap(CONV - 1), tap(CONV), ALU.mult, ALU.add).then_inc(conv_step, 1)
                            for n in range(CONV - 1):
                                lag = CONV - 1 - n
                                rwait(dve, conv_step, j * (2 * NSTEP) + (u * NSTEP + n + 1))
                                dve.scalar_tensor_tensor(
                                    conv[:, u, lag:T], featT[:, ds(j * (2 * T) + (T_MLQ + u) * T, T - lag)],
                                    tap(n), conv[:, u, lag:T], ALU.mult, ALU.add).then_inc(conv_step, 1)
                    with dve.Fori(0, N_FEAT // 2 - N_CONV) as j:
                        for u in range(2):
                            evacuate(j, u, 2 * N_CONV)

        with tensors() as st:
            NZ, NSP, NW = 3, 4, 3
            ks = sb(st, "ks", [P, T])
            qz = sb(st, "qz", [P, 2, T])
            vz = sb(st, "vz", [P, TT, 2, P])
            tri = sb(st, "tri", [P, P])
            zero = sb(st, "zero", [P, P])
            maskw = sb(st, "maskw", [P, NCH])
            zsb = sb(st, "zsb", [P, NZ, NCH])
            spl = sb(st, "spl", [P, NSP, NCH])
            wgt = sb(st, "wgt", [P, NW, NCH])
            acc = sb(st, "acc", [P, 2, 2, NCH])
            zp = ps(st, "zp", [P, 2, NCH])
            rp = ps(st, "rp", [P, 2, NCH])
            yp = ps(st, "yp", [P, TC, NCH])
            QB = NCH // P
            items = [(tc, sbk, lo, h) for tc, sbk, lo in
                     sorted(causal_tiles(), key=lambda a: (a[0], -a[1])) for h in range(2)]
            NI = len(items)
            last_blk = [sbk == (tc + 1) * QB - 1 for tc, sbk, lo, h in items]
            n_acc = [sum(it[1] > 0 for it in items[:n + 1]) for n in range(NI)]
            NA = n_acc[-1]
            opens = {tc: min(n for n in range(NI) if items[n][0] == tc) for tc in range(TC)}
            closes = {tc: max(n for n in range(NI) if items[n][0] == tc) for tc in range(TC)}

            masks_set, in_copied = sem("masks_set"), sem("in_copied")
            z_done, z_copied, z_neg = sem("z_done"), sem("z_copied"), sem("z_neg")
            e_done, l_done, sp_done = sem("e_done"), sem("l_done"), sem("sp_done")
            acc_done, r_done, arg_done = sem("acc_done"), sem("r_done"), sem("arg_done")
            w_done, pv_done, y_stored = sem("w_done"), sem("pv_done"), sem("y_stored")
            N_COPY = 5
            N_MASKS = 6

            with nc.Block() as block:

                @block.gpsimd
                def _(pool):
                    pool.memset(vz[:, :, :, :], 0.0).then_inc(masks_set, 1)
                    pool.memset(zero[:, :], 0.0).then_inc(masks_set, 1)
                    pool.memset(tri[:, :], 1.0).then_inc(masks_set, 1)
                    pool.memset(maskw[:, :], 0.0).then_inc(masks_set, 1)
                    pool.wait_ge(masks_set, 4)
                    pool.affine_select(out=tri[:, :], in_=tri[:, :], compare_op=ALU.is_ge, fill=0.0, base=0,
                                       pattern=[[-1, P]], channel_multiplier=1).then_inc(masks_set, 1)
                    pool.affine_select(out=maskw[:, 0:P], in_=maskw[:, 0:P], compare_op=ALU.is_gt, fill=-BIG, base=0,
                                       pattern=[[1, P]], channel_multiplier=-1).then_inc(masks_set, 1)
                    with pool.Fori(0, PAIRS) as hp:
                        for n, (tc, sbk, lo, h) in enumerate(items):
                            if sbk == 0:
                                continue
                            rwait(pool, sp_done, hp * NI + (n + 1))
                            if n >= 2:
                                rwait(pool, r_done, hp * NI + (n - 1))
                            b = sbk % 2
                            if last_blk[n]:
                                pool.tensor_copy(acc[:, h, b, lo:], spl[:, n % NSP, lo:]).then_inc(acc_done, 1)
                                continue
                            prev = items[n - 2][2]
                            rwait(pool, acc_done, hp * NA + n_acc[n - 2])
                            if prev > lo:
                                pool.tensor_copy(acc[:, h, b, lo:prev], spl[:, n % NSP, lo:prev])
                            pool.tensor_tensor(acc[:, h, b, prev:], acc[:, h, 1 - b, prev:], spl[:, n % NSP, prev:],
                                               ALU.add).then_inc(acc_done, 1)

                @block.tensor
                def _(pe):
                    pe.sem_inc(pv_done, 1)
                    pe.wait_ge(masks_set, N_MASKS)
                    with pe.Fori(0, PAIRS) as hp:
                        pe.wait_ge(in_copied, hp * N_COPY + N_COPY)
                        for i in range(NI + 4):
                            if i < NI:
                                tc, sbk, lo, h = items[i]
                                if i >= 2:
                                    pe.wait_ge(z_copied, hp * NI + (i - 1))
                                pe.matmul(zp[:, i % 2, lo:], ks[:, sbk * P:(sbk + 1) * P],
                                          qz[:, h, tc * NCH + lo:(tc + 1) * NCH], start=True, stop=True).then_inc(z_done, 1)
                            if 2 <= i < NI + 2:
                                n = i - 2
                                tc, sbk, lo, h = items[n]
                                pe.wait_ge(sp_done, hp * NI + (n + 1))
                                if n >= 2:
                                    pe.wait_ge(arg_done, hp * NI + (n - 1))
                                last = pe.matmul(rp[:, n % 2, lo:], tri[:, :], spl[:, n % NSP, lo:],
                                                 start=True, stop=last_blk[n])
                                if not last_blk[n]:
                                    prev = items[n - 2][2]
                                    pe.wait_ge(acc_done, hp * NA + n_acc[n - 2])
                                    last = pe.matmul(rp[:, n % 2, prev:], ones[:, :], acc[:, h, 1 - sbk % 2, prev:],
                                                     start=False, stop=True)
                                last.then_inc(r_done, 1)
                            if i >= 4:
                                n = i - 4
                                tc, sbk, lo, h = items[n]
                                if n == opens[tc]:
                                    pe.wait_ge(y_stored, hp * TC + (tc + 1))
                                    pe.matmul(yp[:, tc, :], zero[:, :], qz[:, 0, 0:NCH], start=True, stop=False)
                                pe.wait_ge(w_done, hp * NI + (n + 1))
                                pe.matmul(yp[:, tc, lo:], vz[:, sbk, h, :], wgt[:, n % NW, lo:],
                                          start=False, stop=n == closes[tc]).then_inc(pv_done, 1)

                @block.scalar
                def _(act):
                    act.sem_inc(y_stored, TC)
                    act.preload_act_table_set("natural_log_exp_and_others")
                    with act.Fori(0, PAIRS) as hp:
                        for i in range(NI + 4):
                            if i < NI:
                                lo = items[i][2]
                                s_ = spl[:, i % NSP, lo:]
                                act.wait_ge(z_neg, hp * NI + (i + 1))
                                act.activation(s_, s_, ACT.Exp).then_inc(e_done, 1)
                                act.wait_ge(e_done, hp * NI + (i + 1))
                                act.activation(s_, s_, ACT.Ln, bias=1.0).then_inc(l_done, 1)
                            if 2 <= i < NI + 2:
                                n = i - 2
                                w_ = wgt[:, n % NW, items[n][2]:]
                                act.wait_ge(arg_done, hp * NI + (n + 1))
                                act.activation(w_, w_, ACT.Exp).then_inc(w_done, 1)
                            for tc in range(TC):
                                if i - 4 == closes[tc]:
                                    rwait(act, pv_done, hp * NI + (closes[tc] + 2))
                                    act.activation(featT[:, ds(hp * T + (T_SBQ * T + tc * NCH), NCH)], yp[:, tc, :],
                                                   ACT.Copy).then_inc(y_stored, 1)

                @block.vector
                def _(dve):
                    dve.wait_ge(masks_set, N_MASKS)
                    with dve.Fori(0, PAIRS) as hp:
                        rwait(dve, pv_done, hp * NI + 1)
                        dve.tensor_copy(ks[:, :], featT[:, ds(hp * T + T_SBK * T, T)]).then_inc(in_copied, 1)
                        for h in range(2):
                            dve.tensor_scalar(qz[:, h, :], featT[:, ds(hp * T + T_SBQ * T, T)],
                                              vec[:, V_HEADMASK + h:V_HEADMASK + h + 1], None, ALU.mult).then_inc(in_copied, 1)
                            dve.tensor_copy(vz[:, :, h, h * SB_DIM:(h + 1) * SB_DIM],
                                            vtok[:, :].rearrange("p (t c) -> p t c", t=TT)[:, :, ds(hp * P + h * SB_DIM, SB_DIM)]
                                            ).then_inc(in_copied, 1)
                        for i in range(NI + 3):
                            if i < NI:
                                tc, sbk, lo, h = items[i]
                                dve.wait_ge(z_done, hp * NI + (i + 1))
                                if i >= 3:
                                    dve.wait_ge(arg_done, hp * NI + (i - 2))
                                if tc * QB <= sbk:
                                    ins = dve.tensor_tensor(zsb[:, i % NZ, lo:], zp[:, i % 2, lo:], maskw[:, 0:NCH - lo], ALU.add)
                                else:
                                    ins = dve.tensor_copy(zsb[:, i % NZ, lo:], zp[:, i % 2, lo:])
                                ins.then_inc(z_copied, 1)
                                dve.wait_ge(z_copied, hp * NI + (i + 1))
                                if i >= NSP:
                                    dve.wait_ge(r_done, hp * NI + (i - NSP + 1))
                                    if items[i - NSP][1] > 0:
                                        dve.wait_ge(acc_done, hp * NA + n_acc[i - NSP])
                                dve.scalar_tensor_tensor(spl[:, i % NSP, lo:], zsb[:, i % NZ, lo:], -1.0, zsb[:, i % NZ, lo:],
                                                         ALU.mult, ALU.min).then_inc(z_neg, 1)
                            if 1 <= i < NI + 1:
                                n = i - 1
                                lo = items[n][2]
                                dve.wait_ge(l_done, hp * NI + (n + 1))
                                dve.scalar_tensor_tensor(spl[:, n % NSP, lo:], zsb[:, n % NZ, lo:], 0.0, spl[:, n % NSP, lo:],
                                                         ALU.max, ALU.add).then_inc(sp_done, 1)
                            if 2 <= i < NI + 2:
                                n = i - 2
                                lo = items[n][2]
                                dve.wait_ge(r_done, hp * NI + (n + 1))
                                if n >= NW:
                                    dve.wait_ge(pv_done, hp * NI + (n - NW + 2))
                                dve.tensor_tensor(wgt[:, n % NW, lo:], zsb[:, n % NZ, lo:], rp[:, n % 2, lo:],
                                                  ALU.subtract).then_inc(arg_done, 1)

        MB0 = T_SBK * T
        KSCALE = float(ML_DIM) ** -0.5
        with tensors() as st:
            acol = sb(st, "acol", [P, ML_HEADS, TT])
            with tensors() as st2:
                rlog = sb(st2, "rlog", [ML_HEADS, T])
                rsum = sb(st2, "rsum", [ML_HEADS, T])
                rmax = sb(st2, "rmax", [ML_HEADS, T])
                rone = sb(st2, "rone", [ML_HEADS, T])
                sel = sb(st2, "sel", [ML_HEADS, ML_HEADS, P])
                ident4 = sb(st2, "ident4", [ML_HEADS, ML_HEADS])
                ap_ = ps(st2, "ap", [P, TT, ML_HEADS])
                bp = ps(st2, "bp", [P, 4, NCH])
                sel_set, row_step = sem("sel_set"), sem("row_step")
                neg_ready, lnf_e, lnf_ready = sem("neg_ready"), sem("lnf_e"), sem("lnf_ready")
                a_ready, acol_done, acol_stored = sem("a_ready"), sem("acol_done"), sem("acol_stored")
                m_ready, bc_done, bc_stored = sem("m_ready"), sem("bc_done"), sem("bc_stored")
                irow, frow = ifrow[:, 0, :], ifrow[:, 1, :]
                bcasts = [(h, c, q) for h in range(ML_HEADS) for c in range(TC) for q in range(2)]

                with nc.Block() as block:

                    @block.gpsimd
                    def _(pool):
                        pool.memset(sel[:, :, :], 1.0).then_inc(sel_set, 1)
                        pool.memset(ident4[:, :], 1.0).then_inc(sel_set, 1)
                        pool.wait_ge(sel_set, 2)
                        pool.affine_select(out=sel[:, :, :], in_=sel[:, :, :], compare_op=ALU.is_equal, fill=0.0, base=0,
                                           pattern=[[-1, ML_HEADS], [0, P]], channel_multiplier=1).then_inc(sel_set, 1)
                        pool.affine_select(out=ident4[:, :], in_=ident4[:, :], compare_op=ALU.is_equal, fill=0.0, base=0,
                                           pattern=[[-1, ML_HEADS]], channel_multiplier=1).then_inc(sel_set, 1)

                    @block.vector
                    def _(dve):
                        dve.memset(rone[:, :], 1.0).then_inc(row_step, 1)
                        dve.scalar_tensor_tensor(rlog[:, :], frow, -1.0, frow, ALU.mult, ALU.min).then_inc(neg_ready, 1)
                        dve.wait_ge(lnf_ready, 1)
                        dve.scalar_tensor_tensor(rlog[:, :], frow, 0.0, rlog[:, :], ALU.min, ALU.subtract).then_inc(row_step, 1)
                        dve.wait_ge(row_step, 2)
                        dve.tensor_tensor_scan(rsum[:, :], rone[:, :], rlog[:, :], 0.0, ALU.mult, ALU.add).then_inc(row_step, 1)
                        dve.wait_ge(row_step, 3)
                        dve.tensor_tensor(irow, irow, rsum[:, :], ALU.subtract).then_inc(a_ready, 1)
                        dve.wait_ge(a_ready, 1)
                        dve.tensor_tensor_scan(rmax[:, :], irow, irow, 0.0, ALU.max, ALU.max).then_inc(row_step, 1)
                        dve.wait_ge(row_step, 4)
                        dve.tensor_tensor(rsum[:, :], rsum[:, :], rmax[:, :], ALU.add).then_inc(m_ready, 1)
                        dve.wait_ge(acol_done, 1)
                        dve.tensor_copy(acol[:, :, :], ap_[:, :, :].rearrange("p t h -> p h t")).then_inc(acol_stored, 1)

                    @block.scalar
                    def _(act):
                        act.preload_act_table_set("natural_log_exp_and_others")
                        act.wait_ge(neg_ready, 1)
                        act.activation(rlog[:, :], rlog[:, :], ACT.Exp).then_inc(lnf_e, 1)
                        act.wait_ge(lnf_e, 1)
                        act.activation(rlog[:, :], rlog[:, :], ACT.Ln, bias=1.0).then_inc(lnf_ready, 1)
                        for n, (h, c, q) in enumerate(bcasts):
                            act.wait_ge(bc_done, n + 1)
                            if q == 0:
                                act.activation(featT[:, MB0 + h * T + c * NCH:MB0 + h * T + (c + 1) * NCH], bp[:, n % 4, :],
                                               ACT.Copy).then_inc(bc_stored, 1)
                            else:
                                at = (h * TC + c) * 2 * NCH
                                act.activation(vtok[:, at:at + NCH], bp[:, n % 4, :], ACT.Exp, scale=-1.0).then_inc(bc_stored, 1)

                    @block.tensor
                    def _(pe):
                        pe.wait_ge(sel_set, 4)
                        pe.wait_ge(a_ready, 1)
                        for t in range(TT):
                            last = pe.matmul(ap_[:, t, :], irow[:, t * P:(t + 1) * P], ident4[:, :], start=True, stop=True)
                        last.then_inc(acol_done, 1)
                        pe.wait_ge(m_ready, 1)
                        for n, (h, c, q) in enumerate(bcasts):
                            if n >= 4:
                                pe.wait_ge(bc_stored, n - 3)
                            row = (rmax, rsum)[q]
                            pe.matmul(bp[:, n % 4, :], sel[:, h, :], row[:, c * NCH:(c + 1) * NCH], start=True, stop=True).then_inc(bc_done, 1)

            with tensors() as st2:
                NE = 3
                km = sb(st2, "km", [P, T])
                qm = sb(st2, "qm", [P, T])
                vm = sb(st2, "vm", [P, TT, P])
                ah = sb(st2, "ah", [P, TT])
                maskm = sb(st2, "maskm", [P, NCH])
                ex = sb(st2, "ex", [P, NE, NCH])
                sw = sb(st2, "sw", [P, NE, NCH])
                fin = sb(st2, "fin", [P, NCH])
                sp_ = ps(st2, "sps", [P, 2, NCH])
                num = ps(st2, "num", [P, TC, NCH])
                den = ps(st2, "den", [P, TC, NCH])
                items = causal_tiles()
                NI = len(items)
                closes = {tc: max(n for n in range(NI) if items[n][0] == tc) for tc in range(TC)}
                QB = NCH // P
                maskm_set, min_copied, mx_done, me_done = sem("maskm_set"), sem("min_copied"), sem("mx_done"), sem("me_done")
                s_done, sw_done, nd_done = sem("s_done"), sem("sw_done"), sem("nd_done")
                den_abs, fin_step, hout_done = sem("den_abs"), sem("fin_step"), sem("hout_done")
                N_COPY = 4

                with nc.Block() as block:

                    @block.gpsimd
                    def _(pool):
                        pool.memset(maskm[:, :], 0.0).then_inc(maskm_set, 1)
                        pool.wait_ge(maskm_set, 1)
                        pool.affine_select(out=maskm[:, 0:P], in_=maskm[:, 0:P], compare_op=ALU.is_ge, fill=BIG, base=0,
                                           pattern=[[1, P]], channel_multiplier=-1).then_inc(maskm_set, 1)

                    @block.tensor
                    def _(pe):
                        pe.sem_inc(nd_done, 1)
                        with pe.Fori(0, ML_HEADS) as h:
                            pe.wait_ge(min_copied, h * N_COPY + N_COPY)
                            for i in range(NI + 2):
                                if i < NI:
                                    tc, sbk, lo = items[i]
                                    if i >= 2:
                                        pe.wait_ge(sw_done, h * NI + (i - 1))
                                    pe.matmul(sp_[:, i % 2, lo:], km[:, sbk * P:(sbk + 1) * P],
                                              qm[:, tc * NCH + lo:(tc + 1) * NCH], start=True, stop=True).then_inc(s_done, 1)
                                if i >= 2:
                                    n = i - 2
                                    tc, sbk, lo = items[n]
                                    if sbk == 0:
                                        pe.wait_ge(hout_done, h * TC + (tc + 1))
                                    pe.wait_ge(sw_done, h * NI + (n + 1))
                                    w_ = sw[:, n % NE, lo:]
                                    pe.matmul(num[:, tc, lo:], vm[:, sbk, :], w_, start=sbk == 0, stop=n == closes[tc])
                                    pe.matmul(den[:, tc, lo:], ones[:, :], w_, start=sbk == 0, stop=n == closes[tc]).then_inc(nd_done, 1)

                    @block.scalar
                    def _(act):
                        with act.Fori(0, ML_HEADS) as h:
                            for i in range(NI + 3):
                                if i < NI:
                                    lo = items[i][2]
                                    act.wait_ge(mx_done, h * NI + (i + 1))
                                    act.activation(ex[:, i % NE, lo:], ex[:, i % NE, lo:], ACT.Exp, scale=-1.0).then_inc(me_done, 1)
                                for tc in range(TC):
                                    if i - 2 == closes[tc]:
                                        act.wait_ge(hout_done, h * TC + (tc + TC))
                                        act.wait_ge(nd_done, h * NI + (closes[tc] + 2))
                                        act.activation(fin[:, :], den[:, tc, :], ACT.Abs).then_inc(den_abs, 1)

                    @block.vector
                    def _(dve):
                        dve.sem_inc(hout_done, TC)
                        dve.wait_ge(maskm_set, 2)
                        with dve.Fori(0, ML_HEADS) as h:
                            rwait(dve, nd_done, h * NI + 1)
                            dve.tensor_copy(km[:, :], featT[:, ds(h * T + T_MLK * T, T)]).then_inc(min_copied, 1)
                            dve.tensor_copy(qm[:, :], featT[:, ds(h * T + T_MLQ * T, T)]).then_inc(min_copied, 1)
                            dve.tensor_copy(vm[:, :, :], vtok[:, :].rearrange("p (t c) -> p t c", t=TT)[:, :, ds(h * P + NCH, P)]
                                            ).then_inc(min_copied, 1)
                            dve.tensor_copy(ah[:, :], acol[:, :, :].rearrange("p h t -> p (h t)")[:, ds(h * TT, TT)]
                                            ).then_inc(min_copied, 1)
                            dve.wait_ge(min_copied, h * N_COPY + N_COPY)
                            for i in range(NI + 4):
                                if i < NI:
                                    tc, sbk, lo = items[i]
                                    m_ = featT[:, ds(h * T + (MB0 + tc * NCH + lo), NCH - lo)]
                                    if i >= NE:
                                        rwait(dve, sw_done, h * NI + (i - NE + 1))
                                    if tc * QB <= sbk:
                                        ins = dve.scalar_tensor_tensor(ex[:, i % NE, lo:], m_, ah[:, sbk:sbk + 1],
                                                                       maskm[:, 0:NCH - lo], ALU.subtract, ALU.max)
                                    else:
                                        ins = dve.tensor_scalar(ex[:, i % NE, lo:], m_, ah[:, sbk:sbk + 1], 0.0,
                                                                ALU.subtract, ALU.max)
                                    ins.then_inc(mx_done, 1)
                                if 1 <= i < NI + 1:
                                    n = i - 1
                                    lo = items[n][2]
                                    dve.wait_ge(s_done, h * NI + (n + 1))
                                    dve.wait_ge(me_done, h * NI + (n + 1))
                                    if n >= NE:
                                        dve.wait_ge(nd_done, h * NI + (n - NE + 2))
                                    dve.scalar_tensor_tensor(sw[:, n % NE, lo:], sp_[:, n % 2, lo:], KSCALE, ex[:, n % NE, lo:],
                                                             ALU.mult, ALU.mult).then_inc(sw_done, 1)
                                for tc in range(TC):
                                    if i - 3 == closes[tc]:
                                        rwait(dve, den_abs, h * TC + (tc + 1))
                                        dve.tensor_tensor(fin[:, :], fin[:, :], vtok[:, ds(h * (TC * 2 * NCH) + tc * 2 * NCH, NCH)],
                                                          ALU.max).then_inc(fin_step, 1)
                                        dve.wait_ge(fin_step, h * (2 * TC) + (2 * tc + 1))
                                        dve.reciprocal(fin[:, :], fin[:, :]).then_inc(fin_step, 1)
                                        rwait(dve, fin_step, h * (2 * TC) + (2 * tc + 2))
                                        dve.tensor_tensor(featT[:, ds(h * T + (T_MLQ * T + tc * NCH), NCH)], num[:, tc, :],
                                                          fin[:, :], ALU.mult).then_inc(hout_done, 1)

            with tensors() as st2:
                hsq = sb(st2, "hsq", [P, 2, T])
                hstd = sb(st2, "hstd", [P, 2, T])
                hs = ps(st2, "hs", [P, 2, TC, NCH])
                osig_done, hsq_done, hs_done, hstd_done = sem("osig_done"), sem("hsq_done"), sem("hs_done"), sem("hstd_done")
                hrec_done, hnorm_done, yml_done = sem("hrec_done"), sem("hnorm_done"), sem("yml_done")

                def tile(k):
                    return featT[:, k * T:(k + 1) * T]

                with nc.Block() as block:

                    @block.scalar
                    def _(act):
                        for h in range(ML_HEADS):
                            act.activation(tile(T_MLO + h), tile(T_MLO + h), ACT.Sigmoid).then_inc(osig_done, 1)
                        for h in range(ML_HEADS):
                            if h >= 2:
                                act.wait_ge(hs_done, h - 1)
                            act.activation(hsq[:, h % 2, :], tile(T_MLQ + h), ACT.Square).then_inc(hsq_done, 1)
                            act.wait_ge(hs_done, h + 1)
                            if h >= 2:
                                act.wait_ge(hnorm_done, h - 1)
                            act.activation(hstd[:, h % 2, :], hs[:, h % 2, :, :].rearrange("p c n -> p (c n)"), ACT.Sqrt,
                                           scale=1.0 / ML_DIM, bias=eps[:, 0:1]).then_inc(hstd_done, 1)

                    @block.tensor
                    def _(pe):
                        for h in range(ML_HEADS):
                            pe.wait_ge(hsq_done, h + 1)
                            if h >= 2:
                                pe.wait_ge(hstd_done, h - 1)
                            for c in range(TC):
                                last = pe.matmul(hs[:, h % 2, c, :], ones[:, :], hsq[:, h % 2, c * NCH:(c + 1) * NCH],
                                                 start=True, stop=True)
                            last.then_inc(hs_done, 1)

                    @block.vector
                    def _(dve):
                        for h in range(ML_HEADS):
                            dve.wait_ge(hstd_done, h + 1)
                            dve.reciprocal(hstd[:, h % 2, :], hstd[:, h % 2, :]).then_inc(hrec_done, 1)
                            dve.wait_ge(hrec_done, h + 1)
                            dve.scalar_tensor_tensor(tile(T_MLQ + h), tile(T_MLQ + h), vec[:, V_MLNORM + h:V_MLNORM + h + 1],
                                                     hstd[:, h % 2, :], ALU.mult, ALU.mult).then_inc(hnorm_done, 1)
                            dve.wait_ge(hnorm_done, h + 1)
                            dve.wait_ge(osig_done, h + 1)
                            dve.tensor_tensor(tile(T_MLQ + h), tile(T_MLQ + h), tile(T_MLO + h), ALU.mult).then_inc(yml_done, 1)
        proj_st.close()

        merged_dram = nc.dram_tensor("merged_scratch", (KD, P, T), F32)
        with tensors() as st:
            NB = SB_HEADS * SB_DIM // P
            NWM = 2 * KD + 2 * NB
            wm = sb(st, "wm", [P, 2, NWM * P])
            sg = sb(st, "sg", [P, TC, 2, NCH])
            br = sb(st, "br", [P, TC, 2, NCH])
            mg = sb(st, "mg", [P, 2, T])
            mp = ps(st, "mp", [P, TC, 4, NCH])
            wm_loaded = [sem(f"wm_loaded{u}") for u in range(2)]
            mg_stored = [sem(f"mg_stored{u}") for u in range(2)]
            mm_done, sg_done, br_done, mg_done = sem("mm_done"), sem("sg_done"), sem("br_done"), sem("mg_done")
            mg_free = sem("mg_free")

            with nc.Block() as block:

                @block.sync
                def _(sp):
                    for u in range(2):
                        sp.dma_start(wm[:, u, :], w_merge[u]).then_inc(wm_loaded[u], 16)

                    def store(j, u, reload):
                        sp.wait_ge(mg_done, j * (2 * TC) + (TC * u + 2 * TC))
                        sp.dma_start(merged_dram[:, :, :].rearrange("n p t -> p n t")[:, ds(j * 2 + u, 1), :],
                                     mg[:, u:u + 1, :]).then_inc(mg_stored[u], 16)
                        if reload:
                            sp.dma_start(wm[:, u:u + 1, :], w_merge.rearrange("n p c -> p n c")[:, ds(j * 2 + (u + 2), 1), :]
                                         ).then_inc(wm_loaded[u], 16)
                        sp.wait_ge(mg_stored[u], j * 16 + 16)
                        sp.sem_inc(mg_free, 1)

                    with sp.Fori(0, KD // 2 - 1) as j:
                        for u in range(2):
                            store(j, u, True)
                    for u in range(2):
                        store(KD // 2 - 1, u, False)

                @block.tensor
                def _(pe):
                    with pe.Fori(0, KD // 2) as j:
                        for u in range(2):
                            pe.wait_ge(wm_loaded[u], j * 16 + 16)
                            for c in range(TC):
                                pe.wait_ge(mg_done, j * 4 + (2 * u + c + 1))
                                at = 0
                                for q, (base, n) in enumerate(((None, KD), (None, KD), (T_SBQ, NB), (T_MLQ, NB))):
                                    for k in range(n):
                                        src = xnT if base is None else featT
                                        col = ((base or 0) + k) * T + c * NCH
                                        last = pe.matmul(mp[:, c, q, :], wm[:, u, (at + k) * P:(at + k + 1) * P],
                                                         src[:, col:col + NCH], start=k == 0, stop=k == n - 1)
                                    at += n
                                last.then_inc(mm_done, 1)

                @block.scalar
                def _(act):
                    with act.Fori(0, KD // 2) as j:
                        for u in range(2):
                            for c in range(TC):
                                act.wait_ge(mm_done, j * 4 + (2 * u + c + 1))
                                act.activation(sg[:, c, :, :], mp[:, c, 0:2, :], ACT.Sigmoid).then_inc(sg_done, 1)

                @block.vector
                def _(dve):
                    dve.sem_inc(mg_done, TC)
                    dve.sem_inc(mg_free, 2)
                    with dve.Fori(0, KD // 2) as j:
                        for u in range(2):
                            for c in range(TC):
                                dve.wait_ge(sg_done, j * 4 + (2 * u + c + 1))
                                dve.tensor_tensor(br[:, c, :, :], sg[:, c, :, :], mp[:, c, 2:4, :], ALU.mult).then_inc(br_done, 1)
                                dve.wait_ge(br_done, j * 4 + (2 * u + c + 1))
                                if c == 0:
                                    dve.wait_ge(mg_free, j * 2 + (u + 1))
                                dve.tensor_tensor(mg[:, u, c * NCH:(c + 1) * NCH], br[:, c, 0, :], br[:, c, 1, :],
                                                  ALU.add).then_inc(mg_done, 1)
        mix_st.close()

        hnT_dram = nc.dram_tensor("hnT_scratch", (TT, P, KD * P), F32)
        peer_st = ctx.enter_context(tensors())
        wq = sb(peer_st, "wq", [P, KD, QT * P])
        kT = sb(peer_st, "kT", [P, QT, P])
        peer_loaded = [sem(f"peer_loaded{n}") for n in range(3)]
        with tensors() as st:
            wo = sb(st, "wo", [P, KD, D])
            nrow = sb(st, "nrow", [P, D])
            mst = sb(st, "mst", [P, 2, KD, P])
            xt = sb(st, "xt", [P, 2, D])
            ht = sb(st, "ht", [P, D])
            hnt = sb(st, "hnt", [P, D])
            hnTt = sb(st, "hnTt", [P, D])
            ident = sb(st, "ident", [P, P])
            ss = sb(st, "ss", [P, 2])
            rs = sb(st, "rs", [P, 1])
            xp = ps(st, "xp", [P, D])
            tp = ps(st, "tp", [P, D])
            wo_loaded, nrow_loaded = sem("wo_loaded"), sem("nrow_loaded")
            m_loaded = [sem(f"m_loaded{u}") for u in range(2)]
            xt_loaded = [sem(f"xt_loaded{u}") for u in range(2)]
            ident_set, mix_done, h_ready, ss_ready, std6_ready = (sem(n) for n in (
                "ident_set", "mix_done", "h_ready", "ss_ready", "std6_ready"))
            rstd6_ready, hn_ready, tp_done, hnT_ready, row_free, hnT_free = (sem(n) for n in (
                "rstd6_ready", "hn_ready", "tp_done", "hnT_ready", "row_free", "hnT_free"))
            h_stored, hn_stored, hnT_stored = sem("h_stored"), sem("hn_stored"), sem("hnT_stored")

            with nc.Block() as block:

                @block.sync
                def _(sp):
                    sp.dma_start(wo[:, :, :], w_out).then_inc(wo_loaded, 16)
                    mv = merged_dram[:, :, :].rearrange("k p t -> p k t")

                    def load_tile(i, u):
                        sp.dma_start(mst[:, u, :, :], mv[:, :, ds(i * P, P)]).then_inc(m_loaded[u], 16)
                        sp.dma_start(xt[:, u, :], x[ds(i * P, P), :]).then_inc(xt_loaded[u], 16)

                    for u in range(2):
                        load_tile(u, u)
                    sp.dma_start(nrow[:, :], rows[0:1, :].broadcast_to([P, D])).then_inc(nrow_loaded, 16)
                    sp.dma_start(wq[:, :, :], w_query).then_inc(peer_loaded[0], 16)
                    sp.dma_start(kT[:, :, :], keysT).then_inc(peer_loaded[1], 16)
                    with sp.Fori(0, TT // 2 - 1) as j:
                        for u in range(2):
                            sp.wait_ge(h_ready, j * 2 + (u + 2))
                            load_tile(j * 2 + (u + 2), u)

                @block.gpsimd
                def _(pool):
                    pool.memset(ident[:, :], 1.0).then_inc(ident_set, 1)
                    pool.wait_ge(ident_set, 1)
                    pool.affine_select(out=ident[:, :], in_=ident[:, :], compare_op=ALU.is_equal, fill=0.0, base=0,
                                       pattern=[[-1, P]], channel_multiplier=1).then_inc(ident_set, 1)
                    with pool.Fori(0, TT) as i:
                        rwait(pool, h_ready, i + 2)
                        pool.dma_start(h_dram[ds(i * P, P), :], ht[:, :]).then_inc(h_stored, 16)
                        rwait(pool, hn_ready, i + 1)
                        pool.dma_start(hn_dram[ds(i * P, P), :], hnt[:, :]).then_inc(hn_stored, 16)
                        rwait(pool, h_stored, i * 16 + 16)
                        rwait(pool, hn_stored, i * 16 + 16)
                        pool.sem_inc(row_free, 1)
                        rwait(pool, hnT_ready, i + 2)
                        pool.dma_start(hnT_dram[:, :, :].rearrange("n p c -> p n c")[:, ds(i, 1), :],
                                       hnTt[:, :].unsqueeze(1)).then_inc(hnT_stored, 16)
                        rwait(pool, hnT_stored, i * 16 + 16)
                        pool.sem_inc(hnT_free, 1)

                @block.tensor
                def _(pe):
                    pe.wait_ge(wo_loaded, 16)
                    pe.wait_ge(ident_set, 2)

                    def mix(i, u, use):
                        pe.wait_ge(m_loaded[u], use * 16 + 16)
                        pe.wait_ge(h_ready, i + 1)
                        for c in range(D // NCH):
                            for k in range(KD):
                                last = pe.matmul(xp[:, c * NCH:(c + 1) * NCH], mst[:, u, k, :], wo[:, k, c * NCH:(c + 1) * NCH],
                                                 start=k == 0, stop=k == KD - 1)
                        last.then_inc(mix_done, 1)

                    def flip(i):
                        pe.wait_ge(hn_ready, i + 1)
                        pe.wait_ge(hnT_ready, i + 1)
                        for k in range(KD):
                            last = pe.transpose(tp[:, k * P:(k + 1) * P], hnt[:, k * P:(k + 1) * P], ident[:, :])
                        last.then_inc(tp_done, 1)

                    mix(0, 0, 0)
                    with pe.Fori(0, TT // 2 - 1) as j:
                        for u in range(2):
                            mix(j * 2 + (u + 1), 1 - u, j + u)
                            flip(j * 2 + u)
                    mix(TT - 1, 1, TT // 2 - 1)
                    for i in (TT - 2, TT - 1):
                        flip(i)

                @block.scalar
                def _(act):
                    with act.Fori(0, TT) as i:
                        act.wait_ge(h_ready, i + 2)
                        act.activation(hnt[:, :], ht[:, :], ACT.Square, accum_out=ss[:, 0:1]).then_inc(ss_ready, 1)
                        act.wait_ge(ss_ready, i + 1)
                        act.activation(ss[:, 1:2], ss[:, 0:1], ACT.Sqrt, scale=1.0 / D, bias=eps[:, 0:1]).then_inc(std6_ready, 1)
                        act.wait_ge(tp_done, i + 1)
                        act.wait_ge(hnT_free, i + 1)
                        act.activation(hnTt[:, :], tp[:, :], ACT.Copy).then_inc(hnT_ready, 1)

                @block.vector
                def _(dve):
                    dve.sem_inc(h_ready, 1)
                    dve.sem_inc(row_free, 1)
                    dve.sem_inc(hnT_free, 1)
                    dve.sem_inc(hnT_ready, 1)
                    dve.wait_ge(nrow_loaded, 16)
                    with dve.Fori(0, TT // 2) as j:
                        for u in range(2):
                            i = j * 2 + u
                            rwait(dve, row_free, i + 1)
                            rwait(dve, xt_loaded[u], j * 16 + 16)
                            rwait(dve, mix_done, i + 1)
                            dve.tensor_tensor(ht[:, :], xt[:, u, :], xp[:, :], ALU.add).then_inc(h_ready, 1)
                            rwait(dve, std6_ready, i + 1)
                            dve.reciprocal(rs[:, :], ss[:, 1:2]).then_inc(rstd6_ready, 1)
                            rwait(dve, rstd6_ready, i + 1)
                            dve.scalar_tensor_tensor(hnt[:, :], ht[:, :], rs[:, 0:1], nrow[:, :], ALU.mult, ALU.mult).then_inc(hn_ready, 1)

        with tensors() as st:
            G, RING = 2, 4
            NGR = NSEL // G
            NJ = NGR // RING
            rowsb = sb(st, "rowsb", [P, RING, G, 2 * D])
            hnT = sb(st, "hnT", [P, KD, P])
            qT = sb(st, "qT", [P, QT, P])
            sc = sb(st, "sc", [P, QT, NKEYS])
            wide = sb(st, "wide", [P, NSEL * TOPK])
            cand = wide[:, :].rearrange("p (h c) -> p h c", h=PH)
            eq = wide[:, :].rearrange("p (n a) -> p n a", a=TOPK)
            v16 = sb(st, "v16", [P, PH, 2, TOPK])
            i16 = sb(st, "i16", [P, PH, 2, TOPK], U32)
            i16f = sb(st, "i16f", [P, PH, 2, TOPK])
            top = sb(st, "top", [P, PH, TOPK])
            topi = sb(st, "topi", [P, PH, TOPK], U32)
            ab = sb(st, "ab", [P, 2, NSEL], U32)
            abf = sb(st, "abf", [P, 2, NSEL])
            esel = sb(st, "esel", [P, 2, NSEL])
            io16 = sb(st, "io16", [P, TOPK])
            e_idx = sb(st, "e_idx", [P, TT * NSEL], I32)
            gate_raw = sb(st, "gate_raw", [P, NSEL])
            gate = sb(st, "gate", [P, NSEL])
            hrow = sb(st, "hrow", [P, D])
            hnrow = sb(st, "hnrow", [P, D])
            hnnext = sb(st, "hnnext", [P, D])
            frow_ = sb(st, "frow", [P, D])
            acc7 = sb(st, "acc7", [P, D])
            idxg = sb(st, "idxg", [P, RING, G], I32)
            gmt = sb(st, "gmt", [P, RING, G])
            dots = sb(st, "dots", [P, RING, G])
            wg = sb(st, "wg", [P, RING, G])
            gs = sb(st, "gs", [P, PH])
            zero7 = sb(st, "zero7", [P, P])
            ident7 = sb(st, "ident7", [P, P])
            diag = sb(st, "diag", [P, RING, G, P])
            yacc = ps(st, "yacc", [P, D])
            ss7 = sb(st, "ss7", [P, 2])
            qp = ps(st, "qp", [P, 4, NCH])
            NG = 4
            GH = QT // NG
            ROUND_Q = 2
            ROUND_TOP = ROUND_Q + NG + 1
            K_STEPS = 16
            hnT_loaded, io_set = sem("hnT_loaded"), sem("io_set")
            q_done, qT_ready, sc_done, sc_stored = (sem(n) for n in ("q_done", "qT_ready", "sc_done", "sc_stored"))
            k_step, sc_read, experts_ready, gexp_done, gate_step = (sem(n) for n in (
                "k_step", "sc_read", "experts_ready", "gexp_done", "gate_step"))
            g_loaded = [[sem(f"g_loaded{r}_{k}") for k in range(G)] for r in range(RING)]
            h7_loaded, hn7_loaded, hn7_copied, f7_loaded = (sem(n) for n in (
                "h7_loaded", "hn7_loaded", "hn7_copied", "f7_loaded"))
            idx_ready, dot_done, gelu_done, wg_done, diag_done = (sem(n) for n in (
                "idx_ready", "dot_done", "gelu_done", "wg_done", "diag_done"))
            sum_done, y7_ready, out_free = sem("sum_done"), sem("y7_ready"), sem("out_free")
            acc_step, ss7_ready, std7_ready, rs7_ready, o7_ready, o7_stored = (sem(n) for n in (
                "acc_step", "ss7_ready", "std7_ready", "rs7_ready", "o7_ready", "o7_stored"))

            with nc.Block() as block:

                @block.sync
                def _(sp):
                    def load_hnT(i):
                        sp.dma_start(hnT[:, :, :].rearrange("p k t -> p (k t)").unsqueeze(1),
                                     hnT_dram[:, :, :].rearrange("n p c -> p n c")[:, ds(i, 1), :]).then_inc(hnT_loaded, 16)

                    def load_h(i):
                        sp.dma_start(hrow[:, :], h_dram[ds(i * P, P), :]).then_inc(h7_loaded, 16)

                    def load_hn(i):
                        sp.dma_start(hnnext[:, :], hn_dram[ds(i * P, P), :]).then_inc(hn7_loaded, 16)

                    def store(i):
                        sp.wait_ge(o7_ready, i + 1)
                        sp.dma_start(out[ds(i * P, P), :], acc7[:, :]).then_inc(o7_stored, 16)

                    load_hnT(0)
                    load_hn(0)
                    load_h(0)
                    sp.dma_start(frow_[:, :], rows[1:2, :].broadcast_to([P, D])).then_inc(f7_loaded, 16)
                    with sp.Fori(0, TT - 1) as i:
                        sp.wait_ge(q_done, i * NG + NG)
                        load_hnT(i + 1)
                        sp.wait_ge(hn7_copied, i + 1)
                        load_hn(i + 1)
                        sp.wait_ge(ss7_ready, i + 1)
                        load_h(i + 1)
                        store(i)
                        sp.wait_ge(o7_stored, i * 16 + 16)
                        sp.sem_inc(out_free, 1)
                    store(TT - 1)
                    sp.wait_ge(o7_stored, TT * 16)

                @block.tensor
                def _(pe):
                    for n in range(2):
                        pe.wait_ge(peer_loaded[n], 16)
                    pe.wait_ge(io_set, 4)

                    def queries(i, g):
                        if g == 0:
                            pe.wait_ge(hnT_loaded, i * 16 + 16)
                        pe.wait_ge(sc_stored, i * NG + (g + 1))
                        for c in range(GH):
                            for k in range(KD):
                                last = pe.matmul(qp[:, g, c * P:(c + 1) * P], wq[:, k, (g * GH + c) * P:(g * GH + c + 1) * P],
                                                 hnT[:, k, :], start=k == 0, stop=k == KD - 1)
                        last.then_inc(q_done, 1)

                    def scores(i):
                        for g in range(NG):
                            pe.wait_ge(qT_ready, i * NG + (g + 1))
                            for c in range(GH):
                                last = pe.matmul(qp[:, g, c * P:(c + 1) * P], qT[:, g * GH + c, :], kT[:, g * GH + c, :],
                                                 start=True, stop=True)
                            last.then_inc(sc_done, 1)

                    def open_sum(i):
                        pe.wait_ge(y7_ready, i + 1)
                        for c in range(D // NCH):
                            pe.matmul(yacc[:, c * NCH:(c + 1) * NCH], zero7[:, :], kT[:, 0:NCH // P, :].rearrange("p a b -> p (a b)"),
                                      start=True, stop=False)

                    def close_sum():
                        for c in range(D // NCH):
                            ins = pe.matmul(yacc[:, c * NCH:(c + 1) * NCH], zero7[:, :], kT[:, 0:NCH // P, :].rearrange("p a b -> p (a b)"),
                                            start=False, stop=True)
                        ins.then_inc(sum_done, 1)

                    def round_(i, j):
                        for r in range(RING):
                            pe.wait_ge(diag_done, i * NGR + j * RING + (r + 1))
                            for k in range(G):
                                for c in range(D // NCH):
                                    ins = pe.matmul(yacc[:, c * NCH:(c + 1) * NCH], diag[:, r, k, :],
                                                    rowsb[:, r, k, D + c * NCH:D + (c + 1) * NCH], start=False, stop=False)
                            ins.then_inc(acc_step, 1)

                    def experts(i, first, last):
                        with pe.Fori(first, last) as j:
                            round_(i, j)

                    for g in range(NG):
                        queries(0, g)
                    scores(0)
                    open_sum(0)
                    round_(0, 0)
                    with pe.Fori(0, TT - 1) as i:
                        for j in range(1, ROUND_Q):
                            round_(i, j)
                        for g in range(NG):
                            queries(i + 1, g)
                            round_(i, ROUND_Q + g)
                        scores(i + 1)
                        experts(i, ROUND_Q + NG, NJ)
                        close_sum()
                        open_sum(i + 1)
                        round_(i + 1, 0)
                    experts(TT - 1, 1, NJ)
                    close_sum()

                @block.gpsimd
                def _(pool):
                    pool.memset(zero7[:, :], 0.0).then_inc(io_set, 1)
                    pool.memset(ident7[:, :], 1.0).then_inc(io_set, 1)
                    pool.iota(io16[:, :], pattern=[[1, TOPK]], base=0, channel_multiplier=0,
                              allow_small_or_imprecise_dtypes=True).then_inc(io_set, 1)
                    pool.wait_ge(io_set, 3)
                    pool.affine_select(out=ident7[:, :], in_=ident7[:, :], compare_op=ALU.is_equal, fill=0.0, base=0,
                                       pattern=[[-1, P]], channel_multiplier=1).then_inc(io_set, 1)
                    with pool.Fori(0, TT) as i:
                        rwait(pool, experts_ready, i + 1)
                        with pool.Fori(0, NJ) as j:
                            for r in range(RING):
                                rwait(pool, acc_step, i * NGR + j * RING + (r + 1))
                                pool.tensor_copy(idxg[:, r, :], e_idx[:, ds(i * NSEL + j * (RING * G) + r * G, G)]).then_inc(idx_ready, 1)
                                rwait(pool, idx_ready, i * NGR + j * RING + (r + 1))
                                for k in range(G):
                                    pool.indirect_dma_start(rowsb[:, r, k, :], None, uv,
                                                            bass.IndirectOffsetOnAxis(ap=idxg[:, r, k:k + 1], axis=0)
                                                            ).then_inc(g_loaded[r][k], 16)

                @block.scalar
                def _(act):
                    act.sem_inc(sc_stored, NG)

                    def queries(i, g):
                        act.wait_ge(q_done, i * NG + (g + 1))
                        act.activation(qT[:, g * GH:(g + 1) * GH, :].rearrange("p c t -> p (c t)"), qp[:, g, :],
                                       ACT.Copy).then_inc(qT_ready, 1)

                    def scores(i):
                        act.wait_ge(sc_read, i + 1)
                        for g in range(NG):
                            act.wait_ge(sc_done, i * NG + (g + 1))
                            act.activation(sc[:, g * GH:(g + 1) * GH, :].rearrange("p c t -> p (c t)"), qp[:, g, :],
                                           ACT.Copy).then_inc(sc_stored, 1)

                    def gates(i):
                        act.wait_ge(experts_ready, i + 1)
                        act.activation(gate[:, :], gate_raw[:, :], ACT.Exp).then_inc(gexp_done, 1)

                    def round_(i, j):
                        def gelu(r):
                            act.wait_ge(dot_done, i * NGR + j * RING + (r + 1))
                            act.activation(gmt[:, r, :], dots[:, r, :], ACT.Gelu).then_inc(gelu_done, 1)

                        def spread(r):
                            act.wait_ge(wg_done, i * NGR + j * RING + (r + 1))
                            for k in range(G):
                                ins = act.activation(diag[:, r, k, :], ident7[:, :], ACT.Copy, scale=wg[:, r, k:k + 1])
                            ins.then_inc(diag_done, 1)

                        gelu(0)
                        for r in range(1, RING):
                            gelu(r)
                            spread(r - 1)
                        spread(RING - 1)

                    def experts(i, first, last):
                        with act.Fori(first, last) as j:
                            round_(i, j)

                    def norm(i):
                        act.wait_ge(y7_ready, i + 2)
                        act.activation(hrow[:, :], acc7[:, :], ACT.Square, accum_out=ss7[:, 0:1]).then_inc(ss7_ready, 1)
                        act.wait_ge(ss7_ready, i + 1)
                        act.activation(ss7[:, 1:2], ss7[:, 0:1], ACT.Sqrt, scale=1.0 / D, bias=eps[:, 0:1]).then_inc(std7_ready, 1)

                    act.wait_ge(io_set, 4)
                    for g in range(NG):
                        queries(0, g)
                    scores(0)
                    gates(0)
                    round_(0, 0)
                    with act.Fori(0, TT - 1) as i:
                        for j in range(1, ROUND_Q):
                            round_(i, j)
                        for g in range(NG):
                            queries(i + 1, g)
                            round_(i, ROUND_Q + g)
                        scores(i + 1)
                        experts(i, ROUND_Q + NG, NJ)
                        gates(i + 1)
                        norm(i)
                        round_(i + 1, 0)
                    experts(TT - 1, 1, NJ)
                    norm(TT - 1)

                @block.vector
                def _(dve):
                    dve.sem_inc(sc_read, 1)
                    dve.sem_inc(acc_step, RING)
                    dve.sem_inc(y7_ready, 1)
                    dve.sem_inc(out_free, 1)
                    dve.wait_ge(io_set, 4)
                    steps = [0]

                    def mark(ins):
                        ins.then_inc(k_step, 1)
                        steps[0] += 1

                    def after_marks(i):
                        rwait(dve, k_step, i * K_STEPS + steps[0])

                    halves = [(h, f) for h in range(PH) for f in range(2)]

                    def top_parts(i):
                        steps[0] = 0
                        rwait(dve, sc_stored, i * NG + 2 * NG)
                        for h, f in halves:
                            last = dve.max(v16[:, h, f, 0:8], sc[:, 2 * h + f, :])
                        mark(last)
                        yield
                        after_marks(i)
                        for h, f in halves:
                            dve.max_index(i16[:, h, f, 0:8], v16[:, h, f, 0:8], sc[:, 2 * h + f, :])
                            last = dve.match_replace(sc[:, 2 * h + f, :], v16[:, h, f, 0:8], sc[:, 2 * h + f, :], NEG)
                        mark(last)
                        yield
                        after_marks(i)
                        for h, f in halves:
                            last = dve.max(v16[:, h, f, 8:16], sc[:, 2 * h + f, :])
                        mark(last)
                        after_marks(i)
                        for h, f in halves:
                            last = dve.max_index(i16[:, h, f, 8:16], v16[:, h, f, 8:16], sc[:, 2 * h + f, :])
                        last.then_inc(sc_read, 1)
                        yield
                        rwait(dve, sc_read, i + 2)
                        dve.tensor_copy(i16f[:, :, :, :], i16[:, :, :, :])
                        mark(dve.tensor_tensor(
                            cand[:, :, :].rearrange("p h (a b) -> p h a b", a=TOPK),
                            v16[:, :, 0, :].unsqueeze(3).broadcast_to([P, PH, TOPK, TOPK]),
                            v16[:, :, 1, :].unsqueeze(2).broadcast_to([P, PH, TOPK, TOPK]), ALU.add))
                        after_marks(i)
                        for h in range(PH):
                            last = dve.max(top[:, h, 0:8], cand[:, h, :])
                        mark(last)
                        yield
                        after_marks(i)
                        for h in range(PH):
                            dve.max_index(topi[:, h, 0:8], top[:, h, 0:8], cand[:, h, :])
                            last = dve.match_replace(cand[:, h, :], top[:, h, 0:8], cand[:, h, :], NEG)
                        mark(last)
                        yield
                        after_marks(i)
                        for h in range(PH):
                            last = dve.max(top[:, h, 8:16], cand[:, h, :])
                        mark(last)
                        after_marks(i)
                        for h in range(PH):
                            last = dve.max_index(topi[:, h, 8:16], top[:, h, 8:16], cand[:, h, :])
                        mark(last)
                        after_marks(i)
                        ti = topi[:, :, :].rearrange("p h k -> p (h k)")
                        dve.tensor_scalar(ab[:, 0, :], ti, 4, None, ALU.logical_shift_right)
                        mark(dve.tensor_scalar(ab[:, 1, :], ti, TOPK - 1, None, ALU.bitwise_and))
                        after_marks(i)
                        mark(dve.tensor_copy(abf[:, :, :], ab[:, :, :]))
                        for f in range(2):
                            yield
                            after_marks(i)
                            mark(dve.tensor_tensor(eq[:, :, :], abf[:, f, :].unsqueeze(2).broadcast_to([P, NSEL, TOPK]),
                                                   io16[:, :].unsqueeze(1).broadcast_to([P, NSEL, TOPK]), ALU.is_equal))
                            after_marks(i)
                            e4 = eq[:, :, :].rearrange("p (h k) a -> p h k a", h=PH)
                            mark(dve.tensor_tensor(e4, e4, i16f[:, :, f, :].unsqueeze(2).broadcast_to([P, PH, TOPK, TOPK]),
                                                   ALU.mult))
                            after_marks(i)
                            last = dve.tensor_reduce(esel[:, f, :], eq[:, :, :], AX.X, ALU.add)
                            mark(last)
                        after_marks(i)
                        dve.scalar_tensor_tensor(e_idx[:, ds(i * NSEL, NSEL)], esel[:, 0, :], float(NKEYS), esel[:, 1, :],
                                                 ALU.mult, ALU.add)
                        dve.tensor_tensor(gate_raw[:, :].rearrange("p (h k) -> p h k", h=PH), top[:, :, :],
                                          top[:, :, 0:1].broadcast_to([P, PH, TOPK]), ALU.subtract).then_inc(experts_ready, 1)
                        assert steps[0] == K_STEPS
                        yield

                    def gates(i):
                        g3 = gate[:, :].rearrange("p (h k) -> p h k", h=PH)
                        rwait(dve, gexp_done, i + 1)
                        dve.tensor_reduce(gs[:, :], g3, AX.X, ALU.add).then_inc(gate_step, 1)
                        rwait(dve, gate_step, i * 3 + 1)
                        dve.reciprocal(gs[:, :], gs[:, :]).then_inc(gate_step, 1)
                        rwait(dve, gate_step, i * 3 + 2)
                        dve.tensor_tensor(g3, g3, gs[:, :].unsqueeze(2).broadcast_to([P, PH, TOPK]), ALU.mult).then_inc(gate_step, 1)
                        rwait(dve, gate_step, i * 3 + 3)

                    def next_hn(i):
                        rwait(dve, hn7_loaded, i * 16 + 16)
                        if not isinstance(i, int):
                            rwait(dve, dot_done, i * NGR)
                        dve.tensor_copy(hnrow[:, :], hnnext[:, :]).then_inc(hn7_copied, 1)
                        rwait(dve, hn7_copied, i + 1)

                    def dot(i, j, r):
                        for k in range(G):
                            rwait(dve, g_loaded[r][k], i * (NJ * 16) + j * 16 + 16)
                            ins = dve.tensor_tensor_reduce(rowsb[:, r, k, 0:D], rowsb[:, r, k, 0:D], hnrow[:, :], 1.0, 0.0,
                                                           ALU.mult, ALU.add, dots[:, r, k:k + 1])
                        ins.then_inc(dot_done, 1)

                    def weigh(i, j, r):
                        rwait(dve, gelu_done, i * NGR + j * RING + (r + 1))
                        dve.tensor_tensor(wg[:, r, :], gmt[:, r, :], gate[:, ds(j * (RING * G) + r * G, G)],
                                          ALU.mult).then_inc(wg_done, 1)

                    def round_(i, j):
                        dot(i, j, 0)
                        for r in range(1, RING):
                            dot(i, j, r)
                            weigh(i, j, r - 1)
                        weigh(i, j, RING - 1)

                    def experts(i, first, last):
                        with dve.Fori(first, last) as j:
                            round_(i, j)

                    def residual(i):
                        rwait(dve, out_free, i + 1)
                        rwait(dve, h7_loaded, i * 16 + 16)
                        rwait(dve, sum_done, i + 1)
                        dve.tensor_tensor(acc7[:, :], hrow[:, :], yacc[:, :], ALU.add).then_inc(y7_ready, 1)

                    def final_norm(i):
                        rwait(dve, std7_ready, i + 1)
                        dve.reciprocal(ss7[:, 0:1], ss7[:, 1:2]).then_inc(rs7_ready, 1)
                        rwait(dve, rs7_ready, i + 1)
                        dve.wait_ge(f7_loaded, 16)
                        dve.scalar_tensor_tensor(acc7[:, :], acc7[:, :], ss7[:, 0:1], frow_[:, :], ALU.mult, ALU.mult).then_inc(o7_ready, 1)

                    for _part in top_parts(0):
                        pass
                    next_hn(0)
                    gates(0)
                    round_(0, 0)
                    with dve.Fori(0, TT - 1) as i:
                        experts(i, 1, ROUND_TOP)
                        j = ROUND_TOP
                        for _part in top_parts(i + 1):
                            round_(i, j)
                            j += 1
                        for j in range(j, NJ):
                            round_(i, j)
                        next_hn(i + 1)
                        residual(i)
                        gates(i + 1)
                        round_(i + 1, 0)
                        final_norm(i)
                    experts(TT - 1, 1, NJ)
                    residual(TT - 1)
                    final_norm(TT - 1)


def kernel(**inputs):
    import concourse.bacc as bacc
    from concourse.bass_utils import run_bass_kernel_spmd

    a = {k: np.asarray(v) for k, v in inputs.items()}
    c = np.ascontiguousarray

    def tiles(w, first, n):
        k = w.shape[0] // P
        return w[:, first:first + n * P].reshape(k, P, n, P).transpose(2, 1, 0, 3).reshape(n, P, k * P)

    w_in = a["w_in"][0]
    sbw, mlw = SB_HEADS * SB_DIM, ML_HEADS * ML_DIM
    o_ml = 3 * sbw
    o_v, o_o = o_ml + 2 * mlw, o_ml + 3 * mlw
    o_if = o_ml + 4 * mlw
    o_g = o_if + 2 * ML_HEADS
    x = a["x"].reshape(T, D)
    w_feat = np.concatenate([tiles(w_in, o_ml, 8), tiles(w_in, o_o, 4), tiles(w_in, 0, 4), tiles(w_in, sbw, 4)])
    w_if = w_in[:, o_if:o_g].reshape(KD, P, 2 * ML_HEADS).transpose(1, 0, 2)
    w_tok = np.concatenate([w_in[:, 2 * sbw:o_ml], w_in[:, o_v:o_o]], axis=1).reshape(KD, P, 2 * NCH).transpose(1, 0, 2)
    w_merge = np.concatenate([tiles(w_in, o_g, KD), tiles(w_in, o_g + D, KD),
                              tiles(a["w_branch_sb"][0], 0, KD), tiles(a["w_branch_ml"][0], 0, KD)], axis=2)
    w_out = a["w_out"][0].reshape(KD, P, D).transpose(1, 0, 2)
    w_query = a["peer_w_query"][0].reshape(KD, P, QT * P).transpose(1, 0, 2)
    keys = np.stack([a["peer_keys1"][0], a["peer_keys2"][0]], axis=1)
    keysT = keys.transpose(3, 0, 1, 2).reshape(P, QT, NKEYS)
    uv = np.concatenate([a["peer_u"][0], a["peer_v"][0]], axis=1)
    rows = np.stack([a["norm_ffn_w"][0], a["norm_final_w"]])

    vecs = np.zeros((P, N_VEC), np.float32)
    vecs[:, V_NORM1:V_NORM1 + KD] = a["norm_mix_w"][0].reshape(KD, P).T
    vecs[:, V_MLNORM:V_MLNORM + ML_HEADS] = a["mlstm_norm_w"][0].reshape(ML_HEADS, P).T
    vecs[:SB_DIM, V_HEADMASK] = SB_DIM ** -0.5
    vecs[SB_DIM:, V_HEADMASK + 1] = SB_DIM ** -0.5
    vecs[:ML_HEADS, V_BI] = a["b_igate"][0]
    vecs[:ML_HEADS, V_BF] = a["b_fgate"][0]
    cv = np.concatenate([a["conv_w"][0], a["conv_b"]], axis=0)
    vecs[:, V_CONV:] = cv.reshape(CONV + 1, N_CONV, P).transpose(2, 1, 0).reshape(P, N_CONV * (CONV + 1))

    arrays = {"xT": x.T, "x_rows": x, "vecs": vecs, "w_feat": w_feat, "w_if": w_if, "w_tok": w_tok, "w_merge": w_merge,
              "w_out_": w_out, "w_query_": w_query, "keysT": keysT, "uv": uv, "rows": rows}
    arrays = {k: c(v) for k, v in arrays.items()}
    nc = bacc.Bacc("TRN2", target_bir_lowering=False, num_devices=1)
    args = [nc.dram_tensor(n, v.shape, mybir.dt.from_np(v.dtype), kind="ExternalInput").ap() for n, v in arrays.items()]
    out = nc.dram_tensor("out", (T, D), F32, kind="ExternalOutput").ap()
    build(nc, *args, out)
    r = run_bass_kernel_spmd(nc, [arrays], core_ids=[0])
    return r.results[0]["out"].reshape(1, T, D)
```
